# Optimizing a Trainium2 kernel written in Bass

```python
import jax, jax.numpy as jnp
from jax import lax
import numpy as np

D_MODEL = 1024
BATCH = 1
SEQ = 256
DEPTH = 1

HA_HEADS = 8
HA_DK = 128
HA_DV = 128
CHUNK = 64
LRU_WIDTH = 1024
LRU_HEADS = 4
LRU_BLOCK = LRU_WIDTH // LRU_HEADS
CONV_WIDTH = 4
RG_C = 8.0
N_EXPERTS = 32
TOP_K = 4
D_FF = 1024
SWIGLU_LIMIT = 7.0
SWIGLU_ALPHA = 1.702
EPS = 1e-5

_IN_SIZES = (HA_HEADS * HA_DK, HA_HEADS * HA_DK, HA_HEADS * HA_DV, HA_HEADS * HA_DV,
             LRU_WIDTH, LRU_WIDTH, D_MODEL, D_MODEL)
IN_COLS = sum(_IN_SIZES)

kernel_name = "hgrn2_rglru_gated_merge_moe_block"

def _split_points():
    return [int(v) for v in np.cumsum(_IN_SIZES)[:-1]]

def rms_norm(x, w):
    xf = x.astype(jnp.float32)
    y = xf * lax.rsqrt(jnp.mean(xf * xf, axis=-1, keepdims=True) + EPS)
    return (y * w.astype(jnp.float32)).astype(x.dtype)

def _to_chunks(t, d):
    b, s = t.shape[:2]
    return t.reshape(b, s // CHUNK, CHUNK, HA_HEADS, d).transpose(0, 3, 1, 2, 4)

def hgrn2_branch(q, f_logit, i_v, g_out, lb, gn_w):
    b, s = q.shape[:2]
    f = lb + (1.0 - lb) * jax.nn.sigmoid(f_logit.astype(jnp.float32))
    log_f = jnp.log(f)
    k = 1.0 - f
    qs = jax.nn.silu(q.astype(jnp.float32))
    q_c, k_c, lf_c = _to_chunks(qs, HA_DK), _to_chunks(k, HA_DK), _to_chunks(log_f, HA_DK)
    v_c = _to_chunks(i_v.astype(jnp.float32), HA_DV)

    bcum = jnp.cumsum(lf_c, axis=3)
    b_last = bcum[:, :, :, -1:, :]
    q_in = q_c * jnp.exp(bcum)
    k_in = k_c * jnp.exp(-bcum)
    k_dec = k_c * jnp.exp(b_last - bcum)

    causal = jnp.tril(jnp.ones((CHUNK, CHUNK), dtype=bool))
    scores = jnp.einsum('bhnid,bhnjd->bhnij', q_in, k_in)
    scores = jnp.where(causal, scores, 0.0)
    o_intra = jnp.einsum('bhnij,bhnjv->bhniv', scores, v_c)

    def chunk_step(state, inp):
        q_n, kd_n, v_n, dec_n = inp
        o_n = jnp.einsum('bhcd,bhdv->bhcv', q_n, state)
        state = dec_n[..., None] * state + jnp.einsum('bhcd,bhcv->bhdv', kd_n, v_n)
        return state, o_n

    xs = (jnp.moveaxis(q_in, 2, 0), jnp.moveaxis(k_dec, 2, 0), jnp.moveaxis(v_c, 2, 0),
          jnp.moveaxis(jnp.exp(b_last[:, :, :, 0, :]), 2, 0))
    state0 = jnp.zeros((b, HA_HEADS, HA_DK, HA_DV), jnp.float32)
    _, o_inter = lax.scan(chunk_step, state0, xs)
    o = o_intra + jnp.moveaxis(o_inter, 0, 2)
    o = o.transpose(0, 2, 3, 1, 4).reshape(b, s, HA_HEADS, HA_DV)
    o = o * lax.rsqrt(jnp.mean(o * o, axis=-1, keepdims=True) + EPS)
    o = o * gn_w.astype(jnp.float32).reshape(HA_HEADS, HA_DV)
    g = jax.nn.silu(g_out.astype(jnp.float32)).reshape(b, s, HA_HEADS, HA_DV)
    return (o * g).reshape(b, s, HA_HEADS * HA_DV)

def _linear_recurrence(c1, c2):
    a1, u1 = c1
    a2, u2 = c2
    return a1 * a2, a2 * u1 + u2

def rglru_branch(xb, gate_b, conv_w, conv_b, w_rg_a, b_rg_a, w_rg_x, b_rg_x, lru_lambda):
    b, s = xb.shape[:2]
    xf = xb.astype(jnp.float32)
    xpad = jnp.pad(xf, ((0, 0), (CONV_WIDTH - 1, 0), (0, 0)))
    cw = conv_w.astype(jnp.float32)
    xc = conv_b.astype(jnp.float32) + sum(xpad[:, k:k + s, :] * cw[k] for k in range(CONV_WIDTH))
    xh = xc.reshape(b, s, LRU_HEADS, LRU_BLOCK)
    r = jax.nn.sigmoid(jnp.einsum('bshi,hij->bshj', xh, w_rg_a.astype(jnp.float32))
                       + b_rg_a.astype(jnp.float32).reshape(LRU_HEADS, LRU_BLOCK))
    ig = jax.nn.sigmoid(jnp.einsum('bshi,hij->bshj', xh, w_rg_x.astype(jnp.float32))
                        + b_rg_x.astype(jnp.float32).reshape(LRU_HEADS, LRU_BLOCK))
    log_a = RG_C * r * jax.nn.log_sigmoid(lru_lambda.astype(jnp.float32)).reshape(LRU_HEADS, LRU_BLOCK)
    a = jnp.exp(log_a)
    mult = jnp.sqrt(-jnp.expm1(2.0 * log_a))
    first = (jnp.arange(s) == 0)[None, :, None, None]
    mult = jnp.where(first, 1.0, mult)
    u = xh * ig * mult
    _, h = lax.associative_scan(_linear_recurrence, (a, u), axis=1)
    return h.reshape(b, s, LRU_WIDTH) * jax.nn.gelu(gate_b.astype(jnp.float32))

def moe_ffn(h, w_router, b_router, w_gu, b_gu, w_down, b_down):
    b, s, d = h.shape
    ht = h.reshape(b * s, d)
    logits = (ht @ w_router + b_router).astype(jnp.float32)
    top_val, top_idx = lax.top_k(logits, TOP_K)
    top_w = jax.nn.softmax(top_val, axis=-1)
    gate = jnp.einsum('tk,tke->te', top_w, jax.nn.one_hot(top_idx, N_EXPERTS, dtype=jnp.float32))
    out = jnp.zeros((b * s, d), jnp.float32)
    for e in range(N_EXPERTS):
        gu = (ht @ w_gu[e] + b_gu[e]).astype(jnp.float32)
        x_glu = jnp.minimum(gu[:, 0::2], SWIGLU_LIMIT)
        x_lin = jnp.clip(gu[:, 1::2], -SWIGLU_LIMIT, SWIGLU_LIMIT)
        act = x_glu * jax.nn.sigmoid(SWIGLU_ALPHA * x_glu) * (x_lin + 1.0)
        y_e = act.astype(ht.dtype) @ w_down[e] + b_down[e]
        out = out + gate[:, e:e + 1] * y_e.astype(jnp.float32)
    return out.reshape(b, s, d)

def setup_inputs(seed: int = 0) -> dict:
    key = jax.random.key(seed)
    ks = jax.random.split(key, 24)
    f32 = jnp.float32
    HK = HA_HEADS * HA_DK
    HV = HA_HEADS * HA_DV

    def nrm(k, shape, scale):
        return jax.random.normal(k, shape, f32) * scale

    a0 = jax.random.uniform(ks[11], (DEPTH, LRU_WIDTH), f32, 0.9, 0.999)
    s0 = a0 ** (1.0 / RG_C)
    lru_lambda = jnp.log(s0) - jnp.log1p(-s0)
    return {
        "x": nrm(ks[0], (BATCH, SEQ, D_MODEL), 1.0),
        "norm_mix": 1.0 + nrm(ks[1], (DEPTH, D_MODEL), 0.02),
        "w_in": nrm(ks[2], (DEPTH, D_MODEL, IN_COLS), D_MODEL ** -0.5),
        "lb_raw": nrm(ks[3], (DEPTH + 1, HK), 0.1),
        "gn_w": 1.0 + nrm(ks[4], (DEPTH, HV), 0.02),
        "conv_w": nrm(ks[5], (DEPTH, CONV_WIDTH, LRU_WIDTH), CONV_WIDTH ** -0.5),
        "conv_b": nrm(ks[6], (DEPTH, LRU_WIDTH), 0.01),
        "w_rg_a": nrm(ks[7], (DEPTH, LRU_HEADS, LRU_BLOCK, LRU_BLOCK), LRU_BLOCK ** -0.5),
        "b_rg_a": nrm(ks[8], (DEPTH, LRU_WIDTH), 0.01),
        "w_rg_x": nrm(ks[9], (DEPTH, LRU_HEADS, LRU_BLOCK, LRU_BLOCK), LRU_BLOCK ** -0.5),
        "b_rg_x": nrm(ks[10], (DEPTH, LRU_WIDTH), 0.01),
        "lru_lambda": lru_lambda,
        "w_proj_a": nrm(ks[12], (DEPTH, HV, D_MODEL), HV ** -0.5),
        "w_proj_b": nrm(ks[13], (DEPTH, LRU_WIDTH, D_MODEL), LRU_WIDTH ** -0.5),
        "w_out": nrm(ks[14], (DEPTH, D_MODEL, D_MODEL), D_MODEL ** -0.5),
        "norm_ffn": 1.0 + nrm(ks[15], (DEPTH, D_MODEL), 0.02),
        "w_router": nrm(ks[16], (DEPTH, D_MODEL, N_EXPERTS), D_MODEL ** -0.5),
        "b_router": nrm(ks[17], (DEPTH, N_EXPERTS), 0.01),
        "w_gu": nrm(ks[18], (DEPTH, N_EXPERTS, D_MODEL, 2 * D_FF), D_MODEL ** -0.5),
        "b_gu": nrm(ks[19], (DEPTH, N_EXPERTS, 2 * D_FF), 0.01),
        "w_down": nrm(ks[20], (DEPTH, N_EXPERTS, D_FF, D_MODEL), D_FF ** -0.5),
        "b_down": nrm(ks[21], (DEPTH, N_EXPERTS, D_MODEL), 0.01),
        "norm_final": 1.0 + nrm(ks[22], (D_MODEL,), 0.02),
    }

def reference(x, norm_mix, w_in, lb_raw, gn_w, conv_w, conv_b, w_rg_a, b_rg_a, w_rg_x, b_rg_x,
              lru_lambda, w_proj_a, w_proj_b, w_out, norm_ffn, w_router, b_router, w_gu, b_gu,
              w_down, b_down, norm_final):
    lower_bounds = jnp.cumsum(jax.nn.softmax(lb_raw.astype(jnp.float32), axis=0), axis=0)
    split_points = _split_points()
    for l in range(DEPTH):
        h = rms_norm(x, norm_mix[l])
        proj = h @ w_in[l]
        q, f_logit, i_v, g_out, xb, gate_b, g_a, g_b = jnp.split(proj, split_points, axis=-1)
        o_a = hgrn2_branch(q, f_logit, i_v, g_out, lower_bounds[l], gn_w[l])
        o_b = rglru_branch(xb, gate_b, conv_w[l], conv_b[l], w_rg_a[l], b_rg_a[l],
                           w_rg_x[l], b_rg_x[l], lru_lambda[l])
        y_a = o_a.astype(x.dtype) @ w_proj_a[l]
        y_b = o_b.astype(x.dtype) @ w_proj_b[l]
        merged = (jax.nn.sigmoid(g_a.astype(jnp.float32)) * y_a.astype(jnp.float32)
                  + jax.nn.sigmoid(g_b.astype(jnp.float32)) * y_b.astype(jnp.float32))
        x = x + (merged.astype(x.dtype) @ w_out[l]).astype(x.dtype)
        h = rms_norm(x, norm_ffn[l])
        x = x + moe_ffn(h, w_router[l], b_router[l], w_gu[l], b_gu[l], w_down[l], b_down[l]).astype(x.dtype)
    return rms_norm(x, norm_final)


_drawn_inputs = setup_inputs


def setup_inputs(seed=0):
    import zlib

    import numpy as np

    out = dict(_drawn_inputs(seed))
    spreads = {}
    factors = {'lb_raw': 4.677,
     'gn_w': 2.864,
     'b_rg_a': 26.421,
     'b_rg_x': 22.068,
     'b_gu': 8.0,
     'b_down': 8.0,
     'norm_final': 7.979}
    for name, (base, spread) in spreads.items():
        noise = np.random.default_rng([zlib.crc32(name.encode()), seed]).standard_normal(out[name].shape)
        drawn = base * np.exp(spread * noise) if base else spread * noise
        out[name] = __import__('jax').numpy.asarray(drawn.astype(out[name].dtype))
    for name, factor in factors.items():
        out[name] = (out[name] * factor).astype(out[name].dtype)
    return out
```

```python
from contextlib import ExitStack

import numpy as np

import concourse.bass as bass
from concourse import mybir

P = 128
D = 1024
T = 256
TA = T // P
KC = D // P
HEADS = 8
CH = 64
NCH = T // CH
LH = 4
LB = 2
NE = 32
TOPK = 4
SLOTS = 64
PASSES = T // SLOTS
LIMIT = 7.0
ALPHA = 1.702
EPS = 1e-5
CONV = 4
RG_C = 8.0

RING = 12
TILE_F = 2048
E_TILES = 12
HG_TILES = 2 * HEADS
LRU_TILES = 3 * LH
MERGE_TILES = 2 * KC
OUT_TILES = 4
MIX_TILES = HG_TILES + LRU_TILES + MERGE_TILES + OUT_TILES
assert MIX_TILES % RING == 0 and E_TILES == RING

C_NMIX, C_NFFN, C_GN, C_CW, C_CB, C_BA, C_BX, C_LAM, C_LB0, C_LB1 = (8 * i for i in (0, 1, 2, 3, 7, 8, 9, 10, 11, 12))
N_VEC = 104
K_ID, K_MEAN, K_RESET, K_IOTA, K_TRI, K_ONE, K_WRAP, K_END = 0, 128, 256, 512, 640, 768, 896, 896 + NE + 1


def build(nc, x, vecs, consts, causal, mixw, w_router, b_router, w_gu, b_gu, w_down, b_down, norm_final, out):
    f32 = mybir.dt.float32
    i32 = mybir.dt.int32
    u32 = mybir.dt.uint32
    ALU = mybir.AluOpType
    ACT = mybir.ActivationFunctionType
    AX = mybir.AxisListType

    ctx = ExitStack()
    with ctx:
        def sb(name, shape, dt=f32):
            return ctx.enter_context(nc.sbuf_tensor(name, shape, dt))

        def sem(name):
            return ctx.enter_context(nc.semaphore(name))

        ring = sb("ring", [P, RING, TILE_F])
        cst = sb("cst", [P, K_END])
        causal_m = sb("causal_m", [P, P], i32)
        vec = sb("vec", [P, N_VEC])
        eps_t = sb("eps_t", [P, 1])
        ident = cst[:, K_ID:K_ID + P]
        mean_m = cst[:, K_MEAN:K_MEAN + P]
        reset_m = cst[:, K_RESET:K_RESET + T]
        iota_m = cst[:, K_IOTA:K_IOTA + P]
        tri_m = cst[:, K_TRI:K_TRI + P]
        ones_m = cst[:, K_ONE:K_ONE + P]
        wrap_m = cst[0:NE, K_WRAP:K_WRAP + NE + 1]

        x_t = sb("x_t", [P, TA, D])
        xn = sb("xn", [P, TA, D])
        hT = sb("hT", [P, KC, T])
        oA = sb("oA", [P, KC, T])
        oB = sb("oB", [P, KC, T])
        merged = sb("merged", [P, KC, T])
        ss = sb("ss", [P, 8])

        PSB = [ctx.enter_context(nc.psum_tensor(f"psb{i}", [P, 512], f32)) for i in range(8)]

        full = [sem(f"ring_full{i}") for i in range(RING)]
        tile_done = sem("tile_done")
        x_in = sem("x_in")
        small_in = sem("small_in")
        causal_in = sem("causal_in")
        late_in = sem("late_in")
        out_done = sem("out_done")

        def slot_of(t):
            return t % RING

        act_step = sem("act_step")
        dve_step = sem("dve_step")
        ssq_ready = sem("ssq_ready")
        xn_ready = sem("xn_ready")
        xT_done = sem("xT_done")
        hT_ready = sem("hT_ready")
        vec_ready = sem("vec_ready")
        lam_y = sem("lam_y")
        first_done = sem("first_done")
        sigq_ready, sigf_ready, sigg_ready = sem("sigq_ready"), sem("sigf_ready"), sem("sigg_ready")
        qs_ready = sem("qs_ready")
        f_ready = sem("f_ready")
        lnf_ready = sem("lnf_ready")
        bcum_ready = sem("bcum_ready")
        exps_ready = sem("exps_ready")
        kq_ready = sem("kq_ready")
        v_ready = sem("v_ready")
        gs_ready = sem("gs_ready")
        st1_done = sem("st1_done")
        sc_ready = sem("sc_ready")
        st2_done = sem("st2_done")
        state_ready = sem("state_ready")
        o_done = sem("o_done")
        osq_ready = sem("osq_ready")
        o_copied = sem("o_copied")
        ms_done = sem("ms_done")
        r_ready = sem("r_ready")
        oA_ready = sem("oA_ready")
        xb_copied = sem("xb_copied")
        xc_ready = sem("xc_ready")
        rsig_ready = sem("rsig_ready")
        tanh_ready = sem("tanh_ready")
        w_ready = sem("w_ready")
        decay_ready = sem("decay_ready")
        mult_ready = sem("mult_ready")
        gsq_ready = sem("gsq_ready")
        garg_ready = sem("garg_ready")
        gsig_ready = sem("gsig_ready")
        oB_ready = sem("oB_ready")
        msig_ready = sem("msig_ready")
        m_ready = sem("m_ready")
        x1_ready = sem("x1_ready")
        lg_done = sem("lg_done")
        negmax_ready = sem("negmax_ready")
        e4_ready = sem("e4_ready")
        mask_ready = sem("mask_ready")
        rank_done = sem("rank_done")
        route_ready = sem("route_ready")
        gateT_done = sem("gateT_done")
        gateT_ready = sem("gateT_ready")
        sel_ready = sem("sel_ready")
        gath_done = sem("gath_done")
        xs_ready = sem("xs_ready")
        moe_step = sem("moe_step")
        glu_ready = sem("glu_ready")
        sig_ready = sem("sig_ready")
        act_ready = sem("act_ready")
        oh_ready = sem("oh_ready")
        actT_done = sem("actT_done")
        actT_ready = sem("actT_ready")
        gsel_ready = sem("gsel_ready")
        gT_done = sem("gT_done")
        gT_ready = sem("gT_ready")
        y_ready = sem("y_ready")
        scat_done = sem("scat_done")
        moe_done = sem("moe_done")
        fin_step = sem("fin_step")
        x2_ready = sem("x2_ready")
        frs_ready = sem("frs_ready")
        fin_ready = sem("fin_ready")

        scr = {}
        names = ("sigq", "sigf", "sigg", "qs", "f", "k", "lnf", "bcum", "dlast", "eb", "enb", "edec", "osq", "rinv")
        hg = sb("hg", [P, len(names), T])
        for i, n in enumerate(names):
            scr[n] = hg[:, i, :]
        msig = [hg[:, 2 * i:2 * i + 2, :].rearrange("p a t -> p (a t)") for i in range(2)]
        q_in, k_in, k_dec = sb("q_in", [P, T]), sb("k_in", [P, T]), sb("k_dec", [P, T])
        gs = [sb(f"gs{i}", [P, T]) for i in range(2)]
        o_sb = [sb(f"o_sb{i}", [P, T]) for i in range(2)]
        v_sb = [sb(f"v_sb{i}", [P, TA, P]) for i in range(2)]
        decs = [sb(f"decs{i}", [P, NCH]) for i in range(2)]
        kdT = sb("kdT", [P, TA, P])
        sc_sb = sb("sc_sb", [P, TA, P])
        S_sb = sb("S_sb", [P, NCH - 1, P])
        dv = sb("dv", [P, 96])
        LBV, OML, C8, NC8, Y8, T0, T1, T2, T3, T4 = (8 * i for i in range(10))
        xpad = sb("xpad", [P, LB, T + CONV - 1])
        xc = sb("xc", [P, LB, T])
        LR = [sb(f"lr{i}", [P, LB, T]) for i in range(8)]
        wr = sb("wr", [P, KC, NE])
        br = sb("br", [P, NE])
        bdn = oA[0:NE, 0:4, :].rearrange("p k t -> p (k t)")
        nfin = oA[:, 4:8, :].rearrange("p k t -> p (k t)")
        bgu = oB[0:NE, :, :].rearrange("p k t -> p (k t)")
        oh = sb("oh", [NE, SLOTS])
        lg = sb("lg", [P, TA, NE])
        top = sb("top", [P, TA, 8])
        topi = sb("topi", [P, TA, 8], u32)
        topf = sb("topf", [P, TA, 8])
        e4 = sb("e4", [P, TA, 8])
        onehot = sb("onehot", [P, NE])
        gate = sb("gate", [P, TA, NE])
        gates = sb("gates", [P, TA, PASSES * NE + 1])
        mask = sb("mask", [P, TA, NE])
        ranks = sb("ranks", [P, TA, PASSES * NE + 1])
        cmax = sb("cmax", [P, 1])
        cnt = sb("cnt", [P, 1], i32)
        gateT = sb("gateT", [NE, T])
        sel = sb("sel", [P, TA, SLOTS])
        gsel = sb("gsel", [P, TA, P])
        xs = LR[4][:, :, :].rearrange("p b n -> p (b n)").rearrange("p (k s) -> p k s", k=KC)
        glu = LR[0][:, :, :].rearrange("p b n -> p (b n)")
        lin = LR[1][:, :, :].rearrange("p b n -> p (b n)")
        sg = LR[5][:, :, :].rearrange("p b n -> p (b n)")
        acT = LR[6][:, :, :].rearrange("p b n -> p (b n)").rearrange("p (c h s) -> p c h s", c=KC // 2, h=2)
        ac = LR[2][:, :, :].rearrange("p b n -> p (b n)")
        gT = sb("gT", [P, T])
        ysb = LR[3][:, :, :].rearrange("p b n -> p (b n)")

        def v1(c):
            return vec[:, c:c + 1]

        def d1(c):
            return dv[:, c:c + 1]

        block = ctx.enter_context(nc.Block())

        @block.sync
        def _(sp):
            sp.dma_start(cst[:, :], consts).then_inc(small_in, 16)
            sp.dma_start(vec[:, :], vecs).then_inc(small_in, 16)
            for t in range(MIX_TILES):
                if t >= RING:
                    sp.wait_ge(tile_done, t - RING + 1)
                sp.dma_start(ring[:, slot_of(t), :], mixw[t]).then_inc(full[slot_of(t)], 16)
            def load_expert(it, e):
                for i in range(E_TILES):
                    sp.wait_ge(tile_done, it * E_TILES + (MIX_TILES - RING + i + 1))
                    src = (w_gu[e, i] if i < KC else
                           w_down[e, 2 * P * (i - KC):2 * P * (i - KC + 1), :].rearrange("(b p) n -> p b n", p=P))
                    dst = ring[:, i, :] if i < KC else ring[:, i, :].rearrange("p (b n) -> p b n", b=2)
                    sp.dma_start(dst, src).then_inc(full[i], 16)

            with sp.Fori(0, NE) as e:
                load_expert(e, e)
            sp.wait_ge(route_ready, 1)
            n = sp.value_load(cnt[0:1, 0:1], min_val=0, max_val=T)
            with sp.If(n > SLOTS):
                with sp.Fori(1, PASSES) as p:
                    with sp.Fori(0, NE) as e:
                        load_expert(p * NE + e, e)
            for a in range(TA):
                sp.wait_ge(fin_ready, a + 1)
                sp.dma_start(out[a * P:(a + 1) * P, :], xn[:, a, :]).then_inc(out_done, 16)
            sp.wait_ge(out_done, 16 * TA)

        @block.gpsimd
        def _(pool):
            pool.dma_start(x_t[:, :, :], x).then_inc(x_in, 16)
            pool.dma_start(causal_m[:, :], causal).then_inc(causal_in, 16)
            pool.dma_start(wr[:, :, :], w_router).then_inc(late_in, 16)
            pool.dma_start(br[:, :], b_router).then_inc(late_in, 16)
            pool.wait_ge(tile_done, MIX_TILES - OUT_TILES)
            pool.dma_start(bdn, b_down).then_inc(late_in, 16)
            pool.dma_start(nfin, norm_final).then_inc(late_in, 16)
            pool.dma_start(bgu, b_gu).then_inc(late_in, 16)

        @block.tensor
        def _(pe):
            def arrived(t):
                pe.wait_ge(full[slot_of(t)], 16 * (t // RING + 1))

            def wblk(t, b, k):
                o = b * D + k * P
                return ring[:, slot_of(t), o:o + P]

            def transposes(src, bank0, first_wait):
                for kb in range(4):
                    if kb >= 2:
                        pe.wait_ge(hT_ready, first_wait + kb - 1)
                    for k2 in range(2):
                        for a in range(TA):
                            k = 2 * kb + k2
                            last = nc.tensor.transpose(PSB[bank0 + kb % 2][:, k2 * T + a * P:k2 * T + (a + 1) * P],
                                                       src[:, a, k * P:(k + 1) * P], ident)
                    last.then_inc(xT_done, 1)

            pe.wait_ge(small_in, 32)
            pe.wait_ge(xn_ready, 2)
            transposes(xn, 0, 0)

            def proj_T(bank, col, t, b, rhs):
                for k in range(KC):
                    last = nc.tensor.matmul(PSB[bank][:, col:col + T], wblk(t, b, k), rhs[:, k, :],
                                            start=(k == 0), stop=(k == KC - 1))
                return last


            pe.wait_ge(hT_ready, 4)
            for h in range(HEADS + 1):
                p = h - 1
                if h < HEADS:
                    arrived(2 * h)
                    if h >= 1:
                        pe.wait_ge(qs_ready, h)
                    proj_T(0, 0, 2 * h, 0, hT).then_inc(first_done, 1)
                if p >= 0:
                    pe.wait_ge(kq_ready, p + 1)
                    if p >= 1:
                        pe.wait_ge(state_ready, p)
                    for a in range(TA):
                        nc.tensor.matmul(PSB[4][:, a * P:(a + 1) * P], k_in[:, a * P:(a + 1) * P],
                                         q_in[:, a * P:(a + 1) * P], start=True, stop=True)
                    for a in range(TA):
                        last = nc.tensor.transpose(PSB[5][:, a * P:(a + 1) * P], k_dec[:, a * P:(a + 1) * P], ident)
                    last.then_inc(st1_done, 1)
                if h < HEADS:
                    if h >= 1:
                        pe.wait_ge(sigf_ready, h)
                    proj_T(1, 0, 2 * h, 1, hT).then_inc(tile_done, 1)
                if p >= 0:
                    pe.wait_ge(sc_ready, p + 1)
                    pe.wait_ge(v_ready, p + 1)
                    for n in range(NCH - 1):
                        a, r = n // 2, CH * (n % 2)
                        bank, col = (4, a * P) if n % 2 == 0 else (5, 0)
                        last = nc.tensor.matmul(PSB[bank][:, col:col + P], kdT[r:r + CH, a, :],
                                                v_sb[p % 2][r:r + CH, a, :], start=True, stop=True)
                    last.then_inc(st2_done, 1)
                if h < HEADS:
                    arrived(2 * h + 1)
                    if h >= 1:
                        pe.wait_ge(v_ready, h)
                    for a in range(TA):
                        for k in range(KC):
                            last = nc.tensor.matmul(PSB[2][:, a * P:(a + 1) * P], hT[:, k, a * P:(a + 1) * P],
                                                    wblk(2 * h + 1, 0, k), start=(k == 0), stop=(k == KC - 1))
                    last.then_inc(first_done, 1)
                if p >= 0:
                    pe.wait_ge(state_ready, p + 1)
                    if p >= 1:
                        pe.wait_ge(osq_ready, p)
                        pe.wait_ge(o_copied, p)
                    for a in range(TA):
                        nc.tensor.matmul(PSB[7][:, a * P:(a + 1) * P], v_sb[p % 2][:, a, :], sc_sb[:, a, :],
                                         start=True, stop=False)
                        for n in (2 * a, 2 * a + 1):
                            if n:
                                last = nc.tensor.matmul(PSB[7][:, n * CH:(n + 1) * CH], S_sb[:, n - 1, :],
                                                        q_in[:, n * CH:(n + 1) * CH], start=False, stop=(n % 2 == 1))
                    last.then_inc(o_done, 1)
                if h < HEADS:
                    if h >= 1:
                        pe.wait_ge(gs_ready, h)
                    proj_T(3, 0, 2 * h + 1, 1, hT).then_inc(tile_done, 1)
                if p >= 0:
                    pe.wait_ge(osq_ready, p + 1)
                    if p >= 1:
                        pe.wait_ge(r_ready, p)
                    nc.tensor.matmul(PSB[6][:, 0:T], mean_m, scr["osq"][:, :], start=True, stop=True).then_inc(ms_done, 1)

            for n in range(LH):
                t = HG_TILES + 3 * n
                arrived(t)
                if n >= 1:
                    pe.wait_ge(xb_copied, n)
                for b in range(LB):
                    last = proj_T(0, b * T, t, b, hT)
                last.then_inc(tile_done, 1)
                arrived(t + 1)
                if n == 0:
                    pe.wait_ge(sigf_ready, HEADS)
                else:
                    pe.wait_ge(oB_ready, n)
                for b in range(LB):
                    last = proj_T(1, b * T, t + 1, b, hT)
                last.then_inc(tile_done, 1)
                arrived(t + 2)
                pe.wait_ge(xc_ready, n + 1)
                if n == 0:
                    pe.wait_ge(gs_ready, HEADS)
                    pe.wait_ge(v_ready, HEADS)
                else:
                    pe.wait_ge(rsig_ready, n)
                for g in range(2):
                    for j in range(LB):
                        for i in range(LB):
                            o = g * 512 + i * T + j * P
                            last = nc.tensor.matmul(PSB[2 + g][:, j * T:(j + 1) * T], ring[:, slot_of(t + 2), o:o + P],
                                                    xc[:, i, :], start=(i == 0), stop=(i == LB - 1))
                last.then_inc(tile_done, 1)

            pe.wait_ge(oA_ready, HEADS)
            for m in range(KC):
                t = HG_TILES + LRU_TILES + 2 * m
                bk = 4 + 2 * (m % 2)
                arrived(t)
                if m == 0:
                    pe.wait_ge(state_ready, HEADS)
                    pe.wait_ge(r_ready, HEADS)
                    pe.wait_ge(o_copied, HEADS)
                if m >= 2:
                    pe.wait_ge(m_ready, m - 1)
                proj_T(bk, 0, t, 0, hT)
                proj_T(bk, T, t, 1, hT).then_inc(tile_done, 1)
                arrived(t + 1)
                if m == 0:
                    pe.wait_ge(oB_ready, LH)
                proj_T(bk + 1, 0, t + 1, 0, oA)
                proj_T(bk + 1, T, t + 1, 1, oB).then_inc(tile_done, 1)

            pe.wait_ge(m_ready, KC)
            pe.wait_ge(rsig_ready, LH)
            for i in range(OUT_TILES):
                t = MIX_TILES - OUT_TILES + i
                arrived(t)
                for k2 in range(2):
                    k = 2 * i + k2
                    for a in range(TA):
                        for n2 in range(2):
                            o = k2 * D + n2 * 512
                            last = nc.tensor.matmul(PSB[2 * a + n2][:, :], merged[:, k, a * P:(a + 1) * P],
                                                    ring[:, slot_of(t), o:o + 512], start=(k == 0), stop=(k == KC - 1))
                last.then_inc(tile_done, 1)

            pe.wait_ge(xn_ready, 4)
            transposes(xn, 4, 4)
            pe.wait_ge(hT_ready, 8)
            pe.wait_ge(late_in, 80)
            for a in range(TA):
                for k in range(KC):
                    last = nc.tensor.matmul(PSB[6][:, a * NE:(a + 1) * NE], hT[:, k, a * P:(a + 1) * P], wr[:, k, :],
                                            start=(k == 0), stop=(k == KC - 1))
            last.then_inc(lg_done, 1)
            pe.wait_ge(mask_ready, 1)
            nc.tensor.matmul(PSB[7][:, 0:NE], tri_m, mask[:, 0, :], start=True, stop=True)
            nc.tensor.matmul(PSB[7][:, NE:2 * NE], ones_m, mask[:, 0, :], start=True, stop=False)
            nc.tensor.matmul(PSB[7][:, NE:2 * NE], tri_m, mask[:, 1, :], start=False, stop=True)
            nc.tensor.matmul(PSB[7][:, 2 * NE:3 * NE], ones_m, mask[:, 0, :], start=True, stop=False)
            nc.tensor.matmul(PSB[7][:, 2 * NE:3 * NE], ones_m, mask[:, 1, :], start=False, stop=True).then_inc(rank_done, 1)
            for a in range(TA):
                last = nc.tensor.transpose(PSB[6][0:NE, 128 + a * P:128 + (a + 1) * P], gate[:, a, :], ident)
            last.then_inc(gateT_done, 1)
            pe.wait_ge(gateT_ready, 1)
            pe.wait_ge(x1_ready, 4)
            for a in range(TA):
                for n2 in range(2):
                    nc.tensor.matmul(PSB[2 * a + n2][:, :], gateT[:, a * P:(a + 1) * P], bdn[:, n2 * 512:(n2 + 1) * 512],
                                     start=True, stop=False, skip_group_check=True)

            def gather(it):
                pe.wait_ge(sel_ready, it + 1)
                for k in range(KC):
                    for a in range(TA):
                        last = nc.tensor.matmul(PSB[7][:, k * SLOTS:(k + 1) * SLOTS], xn[:, a, k * P:(k + 1) * P],
                                                sel[:, a, :], start=(a == 0), stop=(a == TA - 1))
                last.then_inc(gath_done, 1)

            def scatter():
                for a in range(TA):
                    for n2 in range(2):
                        r = n2 * SLOTS
                        last = nc.tensor.matmul(PSB[2 * a + n2][:, :], gT[r:r + SLOTS, a * P:(a + 1) * P],
                                                ysb[r:r + SLOTS, :], start=False, stop=False, skip_group_check=True)
                return last

            def expert(it):
                first = it * E_TILES + (MIX_TILES + 1)
                pe.wait_ge(xs_ready, it + 1)
                pe.wait_ge(oh_ready, it + 1)
                pe.wait_ge(actT_ready, it + 1)
                for g in range(2):
                    for h in range(2):
                        nc.tensor.matmul(PSB[4 + g][h * SLOTS:(h + 1) * SLOTS, :], oh[:, :],
                                         bgu[:, g * D + h * 512:g * D + (h + 1) * 512], start=True, stop=False)
                for k in range(KC):
                    pe.wait_ge(full[k], it * 16 + 16 * (MIX_TILES // RING + 1))
                    for g in range(2):
                        for h in range(2):
                            o = g * D + h * 512
                            last = nc.tensor.matmul(PSB[4 + g][h * SLOTS:(h + 1) * SLOTS, :], xs[:, k, :],
                                                    ring[:, k, o:o + 512], start=False, stop=(k == KC - 1))
                    last.then_inc(tile_done, 1)
                pe.wait_ge(y_ready, it + 1)
                scatter().then_inc(scat_done, 1)
                pe.wait_ge(gsel_ready, it + 1)
                for a in range(TA):
                    last = nc.tensor.transpose(PSB[6][:, a * P:(a + 1) * P], gsel[:, a, :], ident)
                last.then_inc(gT_done, 1)
                gather(it + 1)
                pe.wait_ge(gT_ready, it + 2)
                pe.wait_ge(act_ready, it + 2)
                for c in range(KC // 2):
                    last = nc.tensor.transpose(PSB[4][:, c * P:(c + 1) * P], ac[:, c * P:(c + 1) * P], ident)
                last.then_inc(actT_done, 1)
                pe.wait_ge(actT_ready, it + 2)
                for i in range(E_TILES - KC):
                    pe.wait_ge(full[KC + i], it * 16 + 16 * (MIX_TILES // RING + 1))
                    for k2 in range(2):
                        k = 2 * i + k2
                        for n2 in range(2):
                            o = k2 * D + n2 * 512
                            last = nc.tensor.matmul(PSB[6][n2 * SLOTS:(n2 + 1) * SLOTS, :],
                                                    acT[:, k % 4, k // 4, :], ring[:, KC + i, o:o + 512],
                                                    start=(k == 0), stop=(k == KC - 1))
                    last.then_inc(tile_done, 1)

            gather(0)
            with pe.Fori(0, NE) as e:
                expert(e)
            pe.wait_ge(route_ready, 1)
            n = pe.value_load(cnt[0:1, 0:1], min_val=0, max_val=T)
            with pe.If(n > SLOTS):
                with pe.Fori(1, PASSES) as p:
                    with pe.Fori(0, NE) as e:
                        expert(p * NE + e)
                pe.wait_ge(y_ready, PASSES * NE + 1)
                scatter().then_inc(moe_done, 1)
            with pe.Else():
                pe.wait_ge(y_ready, NE + 1)
                scatter().then_inc(moe_done, 1)

        @block.scalar
        def _(act):
            step = [0]

            def link(ins):
                step[0] += 1
                ins.then_inc(act_step, 1)
                act.wait_ge(act_step, step[0])

            def ln_exp_tables():
                nc.scalar.preload_act_table_set("natural_log_exp_and_others")

            def rstd(src, c, junk):
                for a in range(TA):
                    link(nc.scalar.activation(junk[:, a, :], src[:, a, :], ACT.Square, accum_out=ss[:, c + a:c + a + 1]))
                ln_exp_tables()
                link(nc.scalar.activation(ss[:, c:c + TA], ss[:, c:c + TA], ACT.Ln, scale=1.0 / D, bias=eps_t[:, :]))
                return nc.scalar.activation(ss[:, c:c + TA], ss[:, c:c + TA], ACT.Exp, scale=-0.5)

            act.wait_ge(vec_ready, 1)
            act.wait_ge(x_in, 16)
            rstd(x_t, 0, xn).then_inc(ssq_ready, 1)
            act.wait_ge(vec_ready, 2)
            nc.scalar.activation(dv[:, Y8:Y8 + 8], dv[:, Y8:Y8 + 8], ACT.Exp, scale=-1.0).then_inc(lam_y, 1)
            nc.scalar.activation(dv[:, LBV:LBV + 8], dv[:, LBV:LBV + 8], ACT.Exp, scale=-1.0).then_inc(lam_y, 1)

            S = scr
            for h in range(HEADS + 2):
                p, pp = h - 1, h - 2
                if 0 <= p < HEADS:
                    act.wait_ge(tile_done, 2 * p + 2)
                    if p >= 1:
                        act.wait_ge(gs_ready, p)
                    nc.scalar.activation(S["sigg"][:, :], PSB[3][:, 0:T], ACT.Sigmoid).then_inc(sigg_ready, 1)
                if h < HEADS:
                    act.wait_ge(first_done, 2 * h + 1)
                    if h >= 1:
                        act.wait_ge(qs_ready, h)
                    nc.scalar.activation(S["sigq"][:, :], PSB[0][:, 0:T], ACT.Sigmoid).then_inc(sigq_ready, 1)
                    act.wait_ge(tile_done, 2 * h + 1)
                    if h >= 1:
                        act.wait_ge(f_ready, h)
                    nc.scalar.activation(S["sigf"][:, :], PSB[1][:, 0:T], ACT.Sigmoid).then_inc(sigf_ready, 1)
                ln_exp_tables()
                if h < HEADS:
                    act.wait_ge(f_ready, h + 1)
                    if h >= 1:
                        act.wait_ge(bcum_ready, h)
                    nc.scalar.activation(S["lnf"][:, :], S["f"][:, :], ACT.Ln).then_inc(lnf_ready, 1)
                if pp >= 0:
                    act.wait_ge(ms_done, pp + 1)
                    if pp >= 1:
                        act.wait_ge(oA_ready, pp)
                    link(nc.scalar.activation(S["rinv"][:, :], PSB[6][:, 0:T], ACT.Ln, bias=eps_t[:, :]))
                    nc.scalar.activation(S["rinv"][:, :], S["rinv"][:, :], ACT.Exp, scale=-0.5).then_inc(r_ready, 1)
                if h < HEADS:
                    act.wait_ge(bcum_ready, h + 1)
                    if h >= 1:
                        act.wait_ge(kq_ready, h)
                    nc.scalar.activation(S["eb"][:, :], S["bcum"][:, :], ACT.Exp)
                    nc.scalar.activation(S["enb"][:, :], S["bcum"][:, :], ACT.Exp, scale=-1.0)
                    nc.scalar.activation(S["edec"][:, :], S["dlast"][:, :], ACT.Exp).then_inc(exps_ready, 1)
                    act.wait_ge(first_done, 2 * h + 2)
                    if h >= 2:
                        act.wait_ge(o_done, h - 1)
                    nc.scalar.activation(v_sb[h % 2][:, :, :], PSB[2][:, 0:T].rearrange("p (a n) -> p a n", a=TA),
                                         ACT.Copy).then_inc(v_ready, 1)
                if 0 <= p < HEADS:
                    act.wait_ge(o_done, p + 1)
                    if p >= 1:
                        act.wait_ge(ms_done, p)
                    act.wait_ge(o_copied, p + 1)
                    nc.scalar.activation(S["osq"][:, :], PSB[7][:, 0:T], ACT.Square).then_inc(osq_ready, 1)

            XSQ, ARG, SIG, RS, IG, AD, TH, W = LR
            for n in range(LH):
                t = HG_TILES + 3 * n
                act.wait_ge(tile_done, t + 1)
                if n >= 1:
                    act.wait_ge(xc_ready, n)
                nc.scalar.activation(xpad[:, :, CONV - 1:], PSB[0][:, :].rearrange("p (b n) -> p b n", b=LB),
                                     ACT.Copy).then_inc(xb_copied, 1)
                act.wait_ge(tile_done, t + 2)
                if n >= 1:
                    act.wait_ge(oB_ready, n)
                nc.scalar.activation(XSQ[:, :, :], PSB[1][:, :].rearrange("p (b n) -> p b n", b=LB),
                                     ACT.Square).then_inc(gsq_ready, 1)
                act.wait_ge(tile_done, t + 3)
                for g, (dst, bc) in enumerate(((RS, C_BA), (IG, C_BX))):
                    for j in range(LB):
                        last = nc.scalar.activation(dst[:, j, :], PSB[2 + g][:, j * T:(j + 1) * T], ACT.Sigmoid,
                                                    bias=v1(bc + LB * n + j))
                last.then_inc(rsig_ready, 1)
                act.wait_ge(rsig_ready, n + 1)
                for j in range(LB):
                    last = nc.scalar.activation(TH[:, j, :], RS[:, j, :], ACT.Tanh, scale=d1(NC8 + LB * n + j))
                last.then_inc(tanh_ready, 1)
                act.wait_ge(garg_ready, n + 1)
                nc.scalar.activation(SIG[:, :, :], ARG[:, :, :], ACT.Sigmoid, scale=1.5957691216057308).then_inc(gsig_ready, 1)
                ln_exp_tables()
                for j in range(LB):
                    last = nc.scalar.activation(AD[:, j, :], RS[:, j, :], ACT.Exp, scale=d1(C8 + LB * n + j))
                last.then_inc(decay_ready, 1)
                act.wait_ge(w_ready, n + 1)
                link(nc.scalar.activation(W[:, :, :], W[:, :, :], ACT.Ln))
                nc.scalar.activation(W[:, :, :], W[:, :, :], ACT.Exp, scale=0.5).then_inc(mult_ready, 1)

            for m in range(KC):
                t = HG_TILES + LRU_TILES + 2 * m
                act.wait_ge(tile_done, t + 1)
                if m >= 2:
                    act.wait_ge(m_ready, m - 1)
                nc.scalar.activation(msig[m % 2], PSB[4 + 2 * (m % 2)][:, :], ACT.Sigmoid).then_inc(msig_ready, 1)

            act.wait_ge(x1_ready, 4)
            rstd(x_t, 2, xn).then_inc(ssq_ready, 1)
            act.wait_ge(negmax_ready, 1)
            for a in range(TA):
                last = nc.scalar.activation(e4[:, a, 0:TOPK], top[:, a, 0:TOPK], ACT.Exp, bias=e4[:, a, 4:5],
                                            accum_out=e4[:, a, 5:6])
            last.then_inc(e4_ready, 1)
            act.wait_ge(gateT_done, 1)
            nc.scalar.activation(gateT[:, :], PSB[6][0:NE, 128:128 + T], ACT.Copy).then_inc(gateT_ready, 1)

            def expert(it):
                act.wait_ge(glu_ready, it + 1)
                act.wait_ge(act_ready, it + 1)
                nc.scalar.activation(sg[:, :], glu[:, :], ACT.Sigmoid, scale=ALPHA).then_inc(sig_ready, 1)
                act.wait_ge(gT_done, it + 1)
                nc.scalar.activation(gT[:, :], PSB[6][:, 0:T], ACT.Copy).then_inc(gT_ready, 1)
                act.wait_ge(tile_done, it * E_TILES + (MIX_TILES + E_TILES))
                nc.scalar.activation(ysb[:, :], PSB[6][:, :], ACT.Copy).then_inc(y_ready, 1)

            with act.Fori(0, NE) as e:
                expert(e)
            act.wait_ge(route_ready, 1)
            n = act.value_load(cnt[0:1, 0:1], min_val=0, max_val=T)
            with act.If(n > SLOTS):
                with act.Fori(1, PASSES) as p:
                    with act.Fori(0, NE) as e:
                        expert(p * NE + e)

            act.wait_ge(x2_ready, 4)
            rstd(x_t, 4, xn).then_inc(frs_ready, 1)

        @block.vector
        def _(dve):
            V = nc.vector
            chain = {"sem": dve_step, "n": 0}

            def link(ins):
                chain["n"] += 1
                ins.then_inc(chain["sem"], 1)
                dve.wait_ge(chain["sem"], chain["n"])

            link(V.memset(eps_t[:, :], EPS))
            link(V.memset(sc_sb[:, :, :], 0.0))
            link(V.memset(gT[:, :], 0.0))
            link(V.memset(xpad[:, :, 0:CONV - 1], 0.0))
            link(V.memset(ranks[:, :, PASSES * NE:], -1.0))
            V.memset(gates[:, :, PASSES * NE:], 0.0).then_inc(vec_ready, 1)
            dve.wait_ge(small_in, 32)
            lam = vec[:, C_LAM:C_LAM + 8]
            c8 = lambda c: dv[:, c:c + 8]
            link(V.tensor_scalar(c8(T0), lam, -1.0, None, ALU.mult))
            link(V.tensor_tensor(c8(Y8), lam, c8(T0), ALU.max))
            V.tensor_tensor(c8(LBV), vec[:, C_LB0:C_LB0 + 8], vec[:, C_LB1:C_LB1 + 8], ALU.subtract).then_inc(vec_ready, 1)

            def normed(c, wait):
                dve.wait_ge(ssq_ready, wait)
                for a in range(TA):
                    V.tensor_scalar(xn[:, a, :], x_t[:, a, :], ss[:, c + a:c + a + 1], None, ALU.mult).then_inc(xn_ready, 1)

            def fill_hT(bank0, c_norm, base):
                for kb in range(4):
                    dve.wait_ge(xT_done, base + kb + 1)
                    for k2 in range(2):
                        k = 2 * kb + k2
                        last = V.tensor_scalar(hT[:, k, :], PSB[bank0 + kb % 2][:, k2 * T:(k2 + 1) * T], v1(c_norm + k),
                                               None, ALU.mult)
                    last.then_inc(hT_ready, 1)

            normed(0, 1)
            fill_hT(0, C_NMIX, 0)
            dve.wait_ge(lam_y, 2)
            link(V.tensor_scalar(c8(LBV), c8(LBV), 1.0, None, ALU.add))
            link(V.reciprocal(c8(LBV), c8(LBV)))
            link(V.tensor_scalar(c8(OML), c8(LBV), -1.0, 1.0, ALU.mult, ALU.add))

            dve.wait_ge(causal_in, 16)
            S = scr
            for h in range(HEADS + 2):
                p, pp = h - 1, h - 2
                if 0 <= p < HEADS:
                    dve.wait_ge(sigg_ready, p + 1)
                    if p >= 2:
                        dve.wait_ge(oA_ready, p - 1)
                    V.tensor_tensor(gs[p % 2][:, :], PSB[3][:, 0:T], S["sigg"][:, :], ALU.mult).then_inc(gs_ready, 1)
                if h < HEADS:
                    dve.wait_ge(sigq_ready, h + 1)
                    if h >= 1:
                        dve.wait_ge(kq_ready, h)
                    V.tensor_tensor(S["qs"][:, :], PSB[0][:, 0:T], S["sigq"][:, :], ALU.mult).then_inc(qs_ready, 1)
                if 0 <= p < HEADS:
                    dve.wait_ge(st1_done, p + 1)
                    if p >= 1:
                        dve.wait_ge(o_done, p)
                    for a in range(TA):
                        V.copy_predicated(sc_sb[:, a, :], causal_m[:, :], PSB[4][:, a * P:(a + 1) * P])
                    V.tensor_copy(kdT[:, :, :], PSB[5][:, 0:T].rearrange("p (a n) -> p a n", a=TA)).then_inc(sc_ready, 1)
                if h < HEADS:
                    dve.wait_ge(sigf_ready, h + 1)
                    if h >= 1:
                        dve.wait_ge(lnf_ready, h)
                    V.tensor_scalar(S["f"][:, :], S["sigf"][:, :], d1(OML + h), d1(LBV + h), ALU.mult, ALU.add).then_inc(f_ready, 1)
                    dve.wait_ge(f_ready, h + 1)
                    V.tensor_scalar(S["k"][:, :], S["f"][:, :], -1.0, 1.0, ALU.mult, ALU.add)
                if 0 <= p < HEADS:
                    dve.wait_ge(st2_done, p + 1)
                    link(V.tensor_copy(S_sb[:, 0, :], PSB[4][:, 0:P]))
                    link(V.scalar_tensor_tensor(S_sb[:, 1, :], S_sb[:, 0, :], decs[p % 2][:, 1:2], PSB[5][:, 0:P], ALU.mult, ALU.add))
                    V.scalar_tensor_tensor(S_sb[:, 2, :], S_sb[:, 1, :], decs[p % 2][:, 2:3], PSB[4][:, P:2 * P],
                                           ALU.mult, ALU.add).then_inc(state_ready, 1)
                if h < HEADS:
                    dve.wait_ge(lnf_ready, h + 1)
                    if h >= 1:
                        dve.wait_ge(exps_ready, h)
                    link(V.tensor_tensor_scan(S["bcum"][:, :], reset_m, S["lnf"][:, :], 0.0, ALU.mult, ALU.add))
                    b3 = S["bcum"][:, :].rearrange("p (n c) -> p n c", c=CH)
                    V.tensor_tensor(S["dlast"][:, :].rearrange("p (n c) -> p n c", c=CH),
                                    b3[:, :, CH - 1:CH].to_broadcast([P, NCH, CH]), b3, ALU.subtract).then_inc(bcum_ready, 1)
                if pp >= 0:
                    dve.wait_ge(r_ready, pp + 1)
                    link(V.tensor_tensor(o_sb[pp % 2][:, :], o_sb[pp % 2][:, :], S["rinv"][:, :], ALU.mult))
                    V.scalar_tensor_tensor(oA[:, pp, :], o_sb[pp % 2][:, :], v1(C_GN + pp), gs[pp % 2][:, :],
                                           ALU.mult, ALU.mult).then_inc(oA_ready, 1)
                if h < HEADS:
                    dve.wait_ge(exps_ready, h + 1)
                    if h >= 1:
                        dve.wait_ge(o_done, h) if False else None
                if 0 <= p < HEADS:
                    dve.wait_ge(o_done, p + 1)
                    if p >= 2:
                        dve.wait_ge(oA_ready, p - 1)
                    V.tensor_copy(o_sb[p % 2][:, :], PSB[7][:, 0:T]).then_inc(o_copied, 1)
                if h < HEADS:
                    V.tensor_copy(decs[h % 2][:, :], S["eb"][:, CH - 1::CH])
                    V.tensor_tensor(q_in[:, :], S["qs"][:, :], S["eb"][:, :], ALU.mult)
                    V.tensor_tensor(k_in[:, :], S["k"][:, :], S["enb"][:, :], ALU.mult)
                    V.tensor_tensor(k_dec[:, :], S["k"][:, :], S["edec"][:, :], ALU.mult).then_inc(kq_ready, 1)

            link(V.tensor_scalar(c8(T1), c8(Y8), 2.0, None, ALU.add))
            link(V.reciprocal(c8(T1), c8(T1)))
            link(V.tensor_tensor(c8(T1), c8(Y8), c8(T1), ALU.mult))
            link(V.tensor_tensor(c8(T2), c8(T1), c8(T1), ALU.mult))
            link(V.memset(c8(T3), 1.0 / 17))
            for m in (15, 13, 11, 9, 7, 5, 3, 1):
                link(V.tensor_tensor(c8(T3), c8(T3), c8(T2), ALU.mult))
                link(V.tensor_scalar(c8(T3), c8(T3), 1.0 / m, None, ALU.add))
            link(V.tensor_tensor(c8(T3), c8(T3), c8(T1), ALU.mult))
            link(V.tensor_scalar(c8(T0), c8(T0), 0.0, None, ALU.max))
            link(V.scalar_tensor_tensor(c8(T3), c8(T3), 2.0, c8(T0), ALU.mult, ALU.add))
            link(V.tensor_scalar(c8(NC8), c8(T3), RG_C, None, ALU.mult))
            V.tensor_scalar(c8(C8), c8(T3), -RG_C, None, ALU.mult).then_inc(vec_ready, 1)

            XSQ, ARG, SIG, RS, IG, AD, TH, W = LR
            for n in range(LH):
                t = HG_TILES + 3 * n
                dve.wait_ge(xb_copied, n + 1)
                if n >= 1:
                    dve.wait_ge(tile_done, t)
                for k in range(CONV):
                    for b in range(LB):
                        c = LB * n + b
                        if k == 0:
                            last = V.tensor_scalar(xc[:, b, :], xpad[:, b, 0:T], v1(C_CW + c), v1(C_CB + c), ALU.mult, ALU.add)
                        else:
                            last = V.scalar_tensor_tensor(xc[:, b, :], xpad[:, b, k:k + T], v1(C_CW + 8 * k + c),
                                                          xc[:, b, :], ALU.mult, ALU.add)
                    if k < CONV - 1:
                        link(last)
                    else:
                        last.then_inc(xc_ready, 1)
                gate_ps = PSB[1][:, :].rearrange("p (b n) -> p b n", b=LB)
                dve.wait_ge(gsq_ready, n + 1)
                link(V.tensor_scalar(XSQ[:, :, :], XSQ[:, :, :], 0.044715, 1.0, ALU.mult, ALU.add))
                V.tensor_tensor(ARG[:, :, :], gate_ps, XSQ[:, :, :], ALU.mult).then_inc(garg_ready, 1)
                dve.wait_ge(tanh_ready, n + 1)
                link(V.tensor_scalar(W[:, :, :], TH[:, :, :], 1.0, None, ALU.add))
                link(V.reciprocal(W[:, :, :], W[:, :, :]))
                link(V.scalar_tensor_tensor(W[:, :, :], TH[:, :, :], 2.0, W[:, :, :], ALU.mult, ALU.mult))
                V.tensor_scalar(W[:, :, :], W[:, :, :], 2.0 ** -64, None, ALU.max).then_inc(w_ready, 1)
                dve.wait_ge(gsig_ready, n + 1)
                link(V.tensor_tensor(SIG[:, :, :], gate_ps, SIG[:, :, :], ALU.mult))
                dve.wait_ge(rsig_ready, n + 1)
                link(V.tensor_tensor(IG[:, :, :], xc[:, :, :], IG[:, :, :], ALU.mult))
                dve.wait_ge(mult_ready, n + 1)
                link(V.memset(W[:, :, 0:1], 1.0))
                link(V.tensor_tensor(IG[:, :, :], IG[:, :, :], W[:, :, :], ALU.mult))
                dve.wait_ge(decay_ready, n + 1)
                for j in range(LB):
                    last = V.tensor_tensor_scan(ARG[:, j, :], AD[:, j, :], IG[:, j, :], 0.0, ALU.mult, ALU.add)
                link(last)
                V.tensor_tensor(oB[:, LB * n:LB * (n + 1), :], ARG[:, :, :], SIG[:, :, :], ALU.mult).then_inc(oB_ready, 1)

            for m in range(KC):
                t = HG_TILES + LRU_TILES + 2 * m
                dve.wait_ge(msig_ready, m + 1)
                dve.wait_ge(tile_done, t + 2)
                s2 = msig[m % 2]
                link(V.tensor_tensor(s2, PSB[5 + 2 * (m % 2)][:, :], s2, ALU.mult))
                V.tensor_tensor(merged[:, m, :], s2[:, 0:T], s2[:, T:2 * T], ALU.add).then_inc(m_ready, 1)

            dve.wait_ge(tile_done, MIX_TILES)
            for a in range(TA):
                for n2 in range(2):
                    c = slice(n2 * 512, (n2 + 1) * 512)
                    V.tensor_tensor(x_t[:, a, c], PSB[2 * a + n2][:, :], x_t[:, a, c], ALU.add).then_inc(x1_ready, 1)
            normed(2, 2)
            fill_hT(4, C_NFFN, 4)

            dve.wait_ge(lg_done, 1)
            dve.wait_ge(late_in, 80)
            for a in range(TA):
                link(V.tensor_tensor(lg[:, a, :], PSB[6][:, a * NE:(a + 1) * NE], br[:, :], ALU.add))
                link(V.max(top[:, a, :], lg[:, a, :]))
                link(V.max_index(topi[:, a, :], top[:, a, :], lg[:, a, :]))
                link(V.tensor_copy(topf[:, a, :], topi[:, a, :]))
                link(V.tensor_scalar(e4[:, a, 4:5], top[:, a, 0:1], -1.0, None, ALU.mult))
            V.memset(onehot[:, :], 0.0).then_inc(negmax_ready, 1)
            dve.wait_ge(negmax_ready, 1)
            dve.wait_ge(e4_ready, 1)
            for a in range(TA):
                link(V.reciprocal(e4[:, a, 5:6], e4[:, a, 5:6]))
                link(V.tensor_scalar(e4[:, a, 0:TOPK], e4[:, a, 0:TOPK], e4[:, a, 5:6], None, ALU.mult))
                for k in range(TOPK):
                    tgt = (mask[:, a, :], gate[:, a, :])
                    if k == 0:
                        link(V.tensor_scalar(tgt[0], iota_m[:, 0:NE], topf[:, a, k:k + 1], None, ALU.is_equal))
                        link(V.tensor_scalar(tgt[1], tgt[0], e4[:, a, k:k + 1], None, ALU.mult))
                    else:
                        link(V.tensor_scalar(onehot[:, :], iota_m[:, 0:NE], topf[:, a, k:k + 1], None, ALU.is_equal))
                        link(V.tensor_tensor(tgt[0], tgt[0], onehot[:, :], ALU.add))
                        link(V.scalar_tensor_tensor(tgt[1], onehot[:, :], e4[:, a, k:k + 1], tgt[1], ALU.mult, ALU.add))
            V.tensor_scalar(e4[:, 0, 6:7], e4[:, 0, 5:6], 1.0, None, ALU.mult).then_inc(mask_ready, 1)
            dve.wait_ge(rank_done, 1)
            for a in range(TA):
                r0 = ranks[:, a, 0:NE]
                link(V.scalar_tensor_tensor(r0, PSB[7][:, a * NE:(a + 1) * NE], 1.0, mask[:, a, :], ALU.add, ALU.mult))
                link(V.tensor_scalar(r0, r0, -1.0, None, ALU.add))
                for q in range(1, PASSES):
                    link(V.tensor_scalar(ranks[:, a, q * NE:(q + 1) * NE], r0, float(-SLOTS * q), None, ALU.add))
                for q in range(PASSES):
                    link(V.tensor_copy(gates[:, a, q * NE:(q + 1) * NE], gate[:, a, :]))
            link(V.reduce_max(cmax[:, :], PSB[7][:, 2 * NE:3 * NE], AX.X))
            V.tensor_copy(cnt[:, :], cmax[:, :]).then_inc(route_ready, 1)

            STEPS = 2
            nffn_b = vec[:, C_NFFN:C_NFFN + KC].unsqueeze(2).to_broadcast([P, KC, SLOTS])

            def select(it):
                for a in range(TA):
                    last = V.tensor_scalar(sel[:, a, :], iota_m[:, 0:SLOTS], ranks[:, a, bass.ds(it, 1)], None, ALU.is_equal)
                last.then_inc(sel_ready, 1)

            def take_gathered():
                V.tensor_tensor(xs[:, :, :], PSB[7][:, :].rearrange("p (k s) -> p k s", k=KC), nffn_b,
                                ALU.mult).then_inc(xs_ready, 1)

            def expert(it, e):
                chain = [it * STEPS]

                def link(ins):
                    chain[0] = chain[0] + 1
                    ins.then_inc(moe_step, 1)
                    dve.wait_ge(moe_step, chain[0])

                dve.wait_ge(gT_ready, it + 1)
                for a in range(TA):
                    last = V.tensor_scalar(gsel[:, a, :], iota_m, ranks[:, a, bass.ds(it, 1)],
                                           gates[:, a, bass.ds(it, 1)], ALU.is_equal, ALU.mult)
                last.then_inc(gsel_ready, 1)
                dve.wait_ge(xs_ready, it + 1)
                select(it + 1)
                dve.wait_ge(tile_done, it * E_TILES + (MIX_TILES + KC))
                V.tensor_scalar(glu, PSB[4][:, :], LIMIT, None, ALU.min).then_inc(glu_ready, 1)
                link(V.tensor_scalar(lin, PSB[5][:, :], LIMIT, -LIMIT, ALU.min, ALU.max))
                dve.wait_ge(glu_ready, it + 1)
                link(V.scalar_tensor_tensor(lin, lin, 1.0, glu, ALU.add, ALU.mult))
                dve.wait_ge(sig_ready, it + 1)
                V.tensor_tensor(ac, lin, sg, ALU.mult).then_inc(act_ready, 1)
                V.tensor_scalar(oh[:, :], wrap_m[:, bass.ds(e + 1, 1)].to_broadcast([NE, SLOTS]), 1.0, None,
                                ALU.mult).then_inc(oh_ready, 1)
                dve.wait_ge(actT_done, it + 1)
                V.tensor_copy(acT[:, :, :, :].rearrange("p c h s -> p (c h s)"), PSB[4][:, :]).then_inc(actT_ready, 1)
                dve.wait_ge(gath_done, it + 2)
                take_gathered()

            V.memset(ysb[:, :], 0.0).then_inc(y_ready, 1)
            V.memset(gsel[:, :, :], 0.0).then_inc(gT_ready, 1)
            V.memset(ac, 0.0).then_inc(act_ready, 1)
            V.tensor_copy(oh[:, :], ident[0:NE, 0:1].to_broadcast([NE, SLOTS])).then_inc(oh_ready, 1)
            V.memset(acT[:, :, :, :], 0.0).then_inc(actT_ready, 1)
            select(0)
            dve.wait_ge(gath_done, 1)
            take_gathered()
            with dve.Fori(0, NE) as e:
                expert(e, e)
            dve.wait_ge(route_ready, 1)
            n = dve.value_load(cnt[0:1, 0:1], min_val=0, max_val=T)
            with dve.If(n > SLOTS):
                with dve.Fori(1, PASSES) as p:
                    with dve.Fori(0, NE) as e:
                        expert(p * NE + e, e)

            dve.wait_ge(moe_done, 1)
            for a in range(TA):
                for n2 in range(2):
                    c = slice(n2 * 512, (n2 + 1) * 512)
                    V.tensor_tensor(x_t[:, a, c], PSB[2 * a + n2][:, :], x_t[:, a, c], ALU.add).then_inc(x2_ready, 1)
            dve.wait_ge(frs_ready, 1)
            for a in range(TA):
                V.scalar_tensor_tensor(xn[:, a, :], x_t[:, a, :], ss[:, 4 + a:5 + a], nfin, ALU.mult,
                                       ALU.mult).then_inc(fin_ready, 1)


def constants():
    c = np.zeros((P, K_END), np.float32)
    c[:, K_ID:K_ID + P] = np.eye(P)
    c[:, K_MEAN:K_MEAN + P] = 1.0 / P
    c[:, K_RESET:K_RESET + T] = np.arange(T) % CH != 0
    c[:, K_IOTA:K_IOTA + P] = np.arange(P) % SLOTS
    c[:, K_TRI:K_TRI + P] = np.triu(np.ones((P, P)), 1)
    c[:, K_ONE:K_ONE + P] = 1.0
    c[:NE, K_WRAP:K_WRAP + NE + 1] = np.eye(NE)[:, np.arange(NE + 1) % NE]
    j, i = np.arange(P)[:, None], np.arange(P)[None, :]
    causal = ((i >= j) & (i // CH == j // CH)).astype(np.int32)
    return c, causal


def kernel(**inputs):
    import concourse.bacc as bacc
    from concourse.bass_utils import run_bass_kernel_spmd

    i = {k: np.asarray(v) for k, v in inputs.items()}

    def cols(v):
        return v.reshape(-1, P).T

    vecs = np.concatenate([cols(i[n]) for n in ("norm_mix", "norm_ffn", "gn_w", "conv_w", "conv_b", "b_rg_a", "b_rg_x",
                                                 "lru_lambda", "lb_raw")], axis=1)

    def block(w, c):
        return w[:, c * P:(c + 1) * P].reshape(KC, P, P).transpose(1, 0, 2).reshape(P, D)

    w_in = i["w_in"][0]
    q, f, v, g, xb, gb, ga, gbb = (8 * n for n in range(8))
    tiles = []
    for h in range(HEADS):
        tiles += [(block(w_in, q + h), block(w_in, f + h)), (block(w_in, v + h), block(w_in, g + h))]
    for n in range(LH):
        tiles += [(block(w_in, xb + 2 * n), block(w_in, xb + 2 * n + 1)), (block(w_in, gb + 2 * n), block(w_in, gb + 2 * n + 1))]
        rg = [i[w][0, n].reshape(LB, P, LB * P).transpose(1, 0, 2).reshape(P, 512) for w in ("w_rg_a", "w_rg_x")]
        tiles.append((np.concatenate(rg, axis=1), np.zeros((P, D), np.float32)))
    for m in range(KC):
        tiles += [(block(w_in, ga + m), block(w_in, gbb + m)), (block(i["w_proj_a"][0], m), block(i["w_proj_b"][0], m))]
    for m in range(OUT_TILES):
        w = i["w_out"][0]
        tiles.append((w[2 * m * P:(2 * m + 1) * P], w[(2 * m + 1) * P:(2 * m + 2) * P]))
    mixw = np.stack([np.concatenate(t, axis=1) for t in tiles])

    w_gu = i["w_gu"][0].reshape(NE, KC, P, D, 2).transpose(0, 1, 2, 4, 3).reshape(NE, KC, P, 2 * D)
    b_gu = i["b_gu"][0].reshape(NE, D, 2).transpose(0, 2, 1).reshape(NE, 2 * D)
    consts, causal = constants()
    arrays = {
        "x": i["x"][0].reshape(TA, P, D).transpose(1, 0, 2),
        "vecs": vecs, "consts": consts, "causal": causal, "mixw": mixw,
        "w_router": i["w_router"][0].reshape(KC, P, NE).transpose(1, 0, 2),
        "b_router": np.tile(i["b_router"], (P, 1)),
        "w_gu": w_gu, "b_gu": b_gu, "w_down": i["w_down"][0], "b_down": i["b_down"][0],
        "norm_final": np.tile(i["norm_final"][None], (P, 1)),
    }
    arrays = {f"in_{k}": np.ascontiguousarray(a) for k, a in arrays.items()}
    nc = bacc.Bacc("TRN2", target_bir_lowering=False, num_devices=1)
    args = [nc.dram_tensor(k, a.shape, mybir.dt.from_np(a.dtype), kind="ExternalInput").ap() for k, a in arrays.items()]
    args.append(nc.dram_tensor("out_y", (T, D), mybir.dt.float32, kind="ExternalOutput").ap())
    build(nc, *args)
    r = run_bass_kernel_spmd(nc, [arrays], core_ids=[0])
    return r.results[0]["out_y"].reshape(1, T, D)
```

```python
from contextlib import ExitStack

import numpy as np

import concourse.bass as bass
from concourse import mybir

P = 128
D = 1024
T = 256
TA = T // P
KC = D // P
HEADS = 8
CH = 64
NCH = T // CH
LH = 4
LB = 2
NE = 32
TOPK = 4
SLOTS = 64
PASSES = T // SLOTS
LIMIT = 7.0
ALPHA = 1.702
EPS = 1e-5
CONV = 4
RG_C = 8.0

RING = 12
TILE_F = 2048
E_TILES = 12
HG_TILES = 2 * HEADS
LRU_TILES = 3 * LH
MERGE_TILES = 2 * KC
OUT_TILES = 4
MIX_TILES = HG_TILES + LRU_TILES + MERGE_TILES + OUT_TILES
assert MIX_TILES % RING == 0 and E_TILES == RING

C_NMIX, C_NFFN, C_GN, C_CW, C_CB, C_BA, C_BX, C_LAM, C_LB0, C_LB1 = (8 * i for i in (0, 1, 2, 3, 7, 8, 9, 10, 11, 12))
N_VEC = 104
K_ID, K_MEAN, K_RESET, K_IOTA, K_TRI, K_ONE, K_WRAP, K_END = 0, 128, 256, 512, 640, 768, 896, 896 + NE + 1


ORDER = [("qf", h) if i == 0 else ("vg", h) for h in range(HEADS) for i in range(2)]
ORDER += [("xb", 0), ("gate", 0)]
for _n in range(LH):
    ORDER += [("xb", _n + 1)] * (_n + 1 < LH) + [("rg", _n)] + [("gate", _n + 1)] * (_n + 1 < LH)
for _n in range(KC):
    ORDER += [("mgate", _n), ("mproj", _n)]
ORDER += [("out", _n) for _n in range(OUT_TILES)]
assert len(ORDER) == MIX_TILES
TILE = {name: t for t, name in enumerate(ORDER)}


def build(nc, x, vecs, consts, causal, mixw, w_router, b_router, w_gu, b_gu, w_down, b_down, norm_final, out):
    f32 = mybir.dt.float32
    i32 = mybir.dt.int32
    u32 = mybir.dt.uint32
    ALU = mybir.AluOpType
    ACT = mybir.ActivationFunctionType
    AX = mybir.AxisListType

    ctx = ExitStack()
    with ctx:
        def sb(name, shape, dt=f32):
            return ctx.enter_context(nc.sbuf_tensor(name, shape, dt))

        def sem(name):
            return ctx.enter_context(nc.semaphore(name))

        ring = sb("ring", [P, RING, TILE_F])
        cst = sb("cst", [P, K_END])
        causal_m = sb("causal_m", [P, P], i32)
        vec = sb("vec", [P, N_VEC])
        eps_t = sb("eps_t", [P, 1])
        ident = cst[:, K_ID:K_ID + P]
        mean_m = cst[:, K_MEAN:K_MEAN + P]
        reset_m = cst[:, K_RESET:K_RESET + T]
        iota_m = cst[:, K_IOTA:K_IOTA + P]
        tri_m = cst[:, K_TRI:K_TRI + P]
        ones_m = cst[:, K_ONE:K_ONE + P]
        wrap_m = cst[0:NE, K_WRAP:K_WRAP + NE + 1]

        x_t = sb("x_t", [P, TA, D])
        xn = sb("xn", [P, TA, D])
        hT = sb("hT", [P, KC, T])
        oA = sb("oA", [P, KC, T])
        oB = sb("oB", [P, KC, T])
        merged = sb("merged", [P, KC, T])
        ss = sb("ss", [P, 8])

        PSB = [ctx.enter_context(nc.psum_tensor(f"psb{i}", [P, 512], f32)) for i in range(8)]

        full = [sem(f"ring_full{i}") for i in range(RING)]
        tile_done = sem("tile_done")
        x_in = [sem(f"x_in{a}") for a in range(TA)]
        small_in = sem("small_in")
        causal_in = sem("causal_in")
        late_in = sem("late_in")
        out_done = sem("out_done")

        def slot_of(t):
            return t % RING

        act_step = sem("act_step")
        dve_step = sem("dve_step")
        ssq_ready = sem("ssq_ready")
        xn_ready = sem("xn_ready")
        xT_done = sem("xT_done")
        hT_ready = sem("hT_ready")
        vec_ready = sem("vec_ready")
        lam_y = sem("lam_y")
        first_done = sem("first_done")
        sigq_ready, sigf_ready, sigg_ready = sem("sigq_ready"), sem("sigf_ready"), sem("sigg_ready")
        qs_ready = sem("qs_ready")
        f_ready = sem("f_ready")
        lnf_ready = sem("lnf_ready")
        bcum_ready = sem("bcum_ready")
        exps_ready = sem("exps_ready")
        kq_ready = sem("kq_ready")
        v_ready = sem("v_ready")
        gs_ready = sem("gs_ready")
        st1_done = sem("st1_done")
        sc_ready = sem("sc_ready")
        st2_done = sem("st2_done")
        state_ready = sem("state_ready")
        o_done = sem("o_done")
        osq_ready = sem("osq_ready")
        o_copied = sem("o_copied")
        ms_done = sem("ms_done")
        r_ready = sem("r_ready")
        oA_ready = sem("oA_ready")
        xb_copied = sem("xb_copied")
        xc_ready = sem("xc_ready")
        rsig_ready = sem("rsig_ready")
        tanh_ready = sem("tanh_ready")
        th_ready, lns_ready = sem("th_ready"), sem("lns_ready")
        w_ready = sem("w_ready")
        decay_ready = sem("decay_ready")
        mult_ready = sem("mult_ready")
        gsq_ready = sem("gsq_ready")
        garg_ready = sem("garg_ready")
        gsig_ready = sem("gsig_ready")
        oB_ready = sem("oB_ready")
        msig_ready = sem("msig_ready")
        m_ready = sem("m_ready")
        x1_ready = sem("x1_ready")
        yo_done = sem("yo_done")
        gated = sem("gated")
        lg_done = sem("lg_done")
        negmax_ready = sem("negmax_ready")
        e4_ready = sem("e4_ready")
        mask_ready = sem("mask_ready")
        rank_done = sem("rank_done")
        route_ready = sem("route_ready")
        sel_ready = sem("sel_ready")
        gath_done = sem("gath_done")
        xs_ready = sem("xs_ready")
        moe_step = sem("moe_step")
        glu_ready = sem("glu_ready")
        sig_ready = sem("sig_ready")
        act_ready = sem("act_ready")
        oh_ready = sem("oh_ready")
        actT_done = sem("actT_done")
        actT_ready = sem("actT_ready")
        gsel_ready = sem("gsel_ready")
        gT_done = sem("gT_done")
        gT_ready = sem("gT_ready")
        y_ready = sem("y_ready")
        scat_done = sem("scat_done")
        moe_done = sem("moe_done")
        fin_step = sem("fin_step")
        x2_ready = sem("x2_ready")
        frs_ready = sem("frs_ready")
        fin_ready = sem("fin_ready")

        scr = {}
        names = ("sigq", "sigf", "sigg", "qs", "f", "k", "lnf", "bcum", "dlast", "eb", "enb", "edec", "osq", "rinv")
        hg = sb("hg", [P, len(names), T])
        for i, n in enumerate(names):
            scr[n] = hg[:, i, :]
        msig = [hg[:, 2 * i:2 * i + 2, :].rearrange("p a t -> p (a t)") for i in range(2)]
        q_in, k_in, k_dec = sb("q_in", [P, T]), sb("k_in", [P, T]), sb("k_dec", [P, T])
        gs = [sb(f"gs{i}", [P, T]) for i in range(2)]
        o_sb = [sb(f"o_sb{i}", [P, T]) for i in range(2)]
        v_sb = [sb(f"v_sb{i}", [P, TA, P]) for i in range(2)]
        decs = [sb(f"decs{i}", [P, NCH]) for i in range(2)]
        kdT = sb("kdT", [P, TA, P])
        sc_sb = sb("sc_sb", [P, TA, P])
        S_sb = sb("S_sb", [P, NCH - 1, P])
        dv = sb("dv", [P, 96])
        LBV, OML, C8, NC8, Y8, T0, T1, T2, T3, T4 = (8 * i for i in range(10))
        xpad = sb("xpad", [P, LB, T + CONV - 1])
        xc = [sb(f"xc{i}", [P, LB, T]) for i in range(2)]
        LR = [sb(f"lr{i}", [P, LB, T]) for i in range(8)]
        wr = sb("wr", [P, KC, NE])
        br = sb("br", [P, NE])
        nfin = oA[:, 4:8, :].rearrange("p k t -> p (k t)")
        bgu = oB[0:NE, :, :].rearrange("p k t -> p (k t)")
        oh = sb("oh", [NE, SLOTS])
        lg = sb("lg", [P, TA, NE])
        top = sb("top", [P, TA, 8])
        topi = sb("topi", [P, TA, 8], u32)
        topf = sb("topf", [P, TA, 8])
        e4 = sb("e4", [P, TA, 8])
        oneh = sb("oneh", [P, TOPK, NE])
        gate = sb("gate", [P, TA, NE])
        gates = sb("gates", [P, TA, PASSES * NE + 1])
        mask = sb("mask", [P, TA, NE])
        ranks = sb("ranks", [P, TA, PASSES * NE + 1])
        cmax = sb("cmax", [P, 1])
        cnt = sb("cnt", [P, 1], i32)
        sel = sb("sel", [P, TA, SLOTS])
        gsel = sb("gsel", [P, TA, P])
        junk = hg[:, 4:8, :].rearrange("p a t -> p (a t)")
        xs = LR[4][:, :, :].rearrange("p b n -> p (b n)").rearrange("p (k s) -> p k s", k=KC)
        glu = LR[0][:, :, :].rearrange("p b n -> p (b n)")
        lin = LR[1][:, :, :].rearrange("p b n -> p (b n)")
        sg = LR[5][:, :, :].rearrange("p b n -> p (b n)")
        acT = LR[6][:, :, :].rearrange("p b n -> p (b n)").rearrange("p (c h s) -> p c h s", c=KC // 2, h=2)
        ac = LR[2][:, :, :].rearrange("p b n -> p (b n)")
        gT = sb("gT", [P, T])
        ysb = LR[3][:, :, :].rearrange("p b n -> p (b n)")

        def v1(c):
            return vec[:, c:c + 1]

        def d1(c):
            return dv[:, c:c + 1]

        block = ctx.enter_context(nc.Block())

        @block.sync
        def _(sp):
            for a in range(TA):
                sp.dma_start(x_t[:, a, :], x[:, a, :]).then_inc(x_in[a], 16)
            sp.dma_start(cst[:, :], consts).then_inc(small_in, 16)
            sp.dma_start(vec[:, :], vecs).then_inc(small_in, 16)
            for t in range(MIX_TILES):
                if t >= RING:
                    sp.wait_ge(tile_done, t - RING + 1)
                sp.dma_start(ring[:, slot_of(t), :], mixw[t]).then_inc(full[slot_of(t)], 16)
            def load_expert(it, e):
                for i in range(E_TILES):
                    sp.wait_ge(tile_done, it * E_TILES + (MIX_TILES - RING + i + 1))
                    src = (w_gu[e, i] if i < KC else
                           w_down[e, 2 * P * (i - KC):2 * P * (i - KC + 1), :].rearrange("(b p) n -> p b n", p=P))
                    dst = ring[:, i, :] if i < KC else ring[:, i, :].rearrange("p (b n) -> p b n", b=2)
                    sp.dma_start(dst, src).then_inc(full[i], 16)

            with sp.Fori(0, NE) as e:
                load_expert(e, e)
            sp.wait_ge(route_ready, 1)
            n = sp.value_load(cnt[0:1, 0:1], min_val=0, max_val=T)
            with sp.If(n > SLOTS):
                with sp.Fori(1, PASSES) as p:
                    with sp.Fori(0, NE) as e:
                        load_expert(p * NE + e, e)
            for a in range(TA):
                sp.wait_ge(fin_ready, a + 1)
                sp.dma_start(out[a * P:(a + 1) * P, :], xn[:, a, :]).then_inc(out_done, 16)
            sp.wait_ge(out_done, 16 * TA)

        @block.gpsimd
        def _(pool):
            pool.dma_start(causal_m[:, :], causal).then_inc(causal_in, 16)
            pool.dma_start(wr[:, :, :], w_router).then_inc(late_in, 16)
            pool.dma_start(br[:, :], b_router).then_inc(late_in, 16)
            pool.wait_ge(tile_done, MIX_TILES - OUT_TILES)
            pool.dma_start(ysb, b_down).then_inc(late_in, 16)
            pool.dma_start(nfin, norm_final).then_inc(late_in, 16)
            pool.dma_start(bgu, b_gu).then_inc(late_in, 16)

        @block.tensor
        def _(pe):
            def arrived(t):
                pe.wait_ge(full[slot_of(t)], 16 * (t // RING + 1))

            def wblk(t, b, k):
                o = b * D + k * P
                return ring[:, slot_of(t), o:o + P]

            def transposes(a, bank0):
                for kb in range(2):
                    for k4 in range(4):
                        k = 4 * kb + k4
                        last = nc.tensor.transpose(PSB[bank0 + kb][:, k4 * P:(k4 + 1) * P], xn[:, a, k * P:(k + 1) * P],
                                                   ident)
                    last.then_inc(xT_done, 1)

            pe.wait_ge(small_in, 32)
            for a in range(TA):
                pe.wait_ge(xn_ready, a + 1)
                transposes(a, 4 + 2 * a)

            def proj_T(bank, col, t, b, rhs):
                for k in range(KC):
                    last = nc.tensor.matmul(PSB[bank][:, col:col + T], wblk(t, b, k), rhs[:, k, :],
                                            start=(k == 0), stop=(k == KC - 1))
                return last


            pe.wait_ge(hT_ready, 4)
            for h in range(HEADS + 1):
                p = h - 1
                if h < HEADS:
                    arrived(2 * h)
                    if h >= 1:
                        pe.wait_ge(qs_ready, h)
                    proj_T(0, 0, 2 * h, 0, hT).then_inc(first_done, 1)
                else:
                    arrived(TILE["xb", 0])
                    pe.wait_ge(qs_ready, HEADS)
                    proj_T(0, 0, TILE["xb", 0], 0, hT)
                if p >= 0:
                    pe.wait_ge(kq_ready, p + 1)
                    if p >= 1:
                        pe.wait_ge(state_ready, p)
                    for a in range(TA):
                        nc.tensor.matmul(PSB[4][:, a * P:(a + 1) * P], k_in[:, a * P:(a + 1) * P],
                                         q_in[:, a * P:(a + 1) * P], start=True, stop=True)
                    for a in range(TA):
                        last = nc.tensor.transpose(PSB[5][:, a * P:(a + 1) * P], k_dec[:, a * P:(a + 1) * P], ident)
                    last.then_inc(st1_done, 1)
                if h < HEADS:
                    if h >= 1:
                        pe.wait_ge(sigf_ready, h)
                    proj_T(1, 0, 2 * h, 1, hT).then_inc(tile_done, 1)
                else:
                    proj_T(0, T, TILE["xb", 0], 1, hT).then_inc(tile_done, 1)
                if p >= 0:
                    pe.wait_ge(sc_ready, p + 1)
                    pe.wait_ge(v_ready, p + 1)
                    for n in range(NCH - 1):
                        a, r = n // 2, CH * (n % 2)
                        bank, col = (4, a * P) if n % 2 == 0 else (5, 0)
                        last = nc.tensor.matmul(PSB[bank][:, col:col + P], kdT[r:r + CH, a, :],
                                                v_sb[p % 2][r:r + CH, a, :], start=True, stop=True)
                    last.then_inc(st2_done, 1)
                if h < HEADS:
                    arrived(2 * h + 1)
                    if h >= 1:
                        pe.wait_ge(v_ready, h)
                    for a in range(TA):
                        for k in range(KC):
                            last = nc.tensor.matmul(PSB[2][:, a * P:(a + 1) * P], hT[:, k, a * P:(a + 1) * P],
                                                    wblk(2 * h + 1, 0, k), start=(k == 0), stop=(k == KC - 1))
                    last.then_inc(first_done, 1)
                else:
                    arrived(TILE["gate", 0])
                    pe.wait_ge(sigf_ready, HEADS)
                    proj_T(1, 0, TILE["gate", 0], 0, hT)
                if p >= 0:
                    pe.wait_ge(state_ready, p + 1)
                    if p >= 1:
                        pe.wait_ge(osq_ready, p)
                        pe.wait_ge(o_copied, p)
                    for a in range(TA):
                        nc.tensor.matmul(PSB[7][:, a * P:(a + 1) * P], v_sb[p % 2][:, a, :], sc_sb[:, a, :],
                                         start=True, stop=False)
                        for n in (2 * a, 2 * a + 1):
                            if n:
                                last = nc.tensor.matmul(PSB[7][:, n * CH:(n + 1) * CH], S_sb[:, n - 1, :],
                                                        q_in[:, n * CH:(n + 1) * CH], start=False, stop=(n % 2 == 1))
                    last.then_inc(o_done, 1)
                if h < HEADS:
                    if h >= 1:
                        pe.wait_ge(gs_ready, h)
                    proj_T(3, 0, 2 * h + 1, 1, hT).then_inc(tile_done, 1)
                else:
                    proj_T(1, T, TILE["gate", 0], 1, hT).then_inc(tile_done, 1)
                if p >= 0:
                    pe.wait_ge(osq_ready, p + 1)
                    if p >= 1:
                        pe.wait_ge(r_ready, p)
                    nc.tensor.matmul(PSB[6][:, 0:T], mean_m, scr["osq"][:, :], start=True, stop=True).then_inc(ms_done, 1)

            def two_blocks(bank, t):
                arrived(t)
                proj_T(bank, 0, t, 0, hT)
                proj_T(bank, T, t, 1, hT).then_inc(tile_done, 1)

            for n in range(LH):
                bk, nbk = 4 * (n % 2), 4 * ((n + 1) % 2)
                if n + 1 < LH:
                    if n == 0:
                        pe.wait_ge(state_ready, HEADS)
                        pe.wait_ge(o_copied, HEADS)
                    else:
                        pe.wait_ge(xb_copied, n)
                    two_blocks(nbk, TILE["xb", n + 1])
                t = TILE["rg", n]
                arrived(t)
                pe.wait_ge(xc_ready, n + 1)
                if n == 0:
                    pe.wait_ge(gs_ready, HEADS)
                    pe.wait_ge(v_ready, HEADS)
                elif n == 1:
                    pe.wait_ge(r_ready, HEADS)
                    pe.wait_ge(osq_ready, HEADS)
                else:
                    pe.wait_ge(rsig_ready, n - 1)
                for g in range(2):
                    for j in range(LB):
                        for i in range(LB):
                            o = g * 512 + i * T + j * P
                            last = nc.tensor.matmul(PSB[bk + 2 + g][:, j * T:(j + 1) * T], ring[:, slot_of(t), o:o + P],
                                                    xc[n % 2][:, i, :], start=(i == 0), stop=(i == LB - 1))
                last.then_inc(tile_done, 1)
                if n + 1 < LH:
                    if n >= 1:
                        pe.wait_ge(oB_ready, n)
                    two_blocks(nbk + 1, TILE["gate", n + 1])

            pe.wait_ge(oA_ready, HEADS)
            pe.wait_ge(oB_ready, LH - 1)
            for m in range(KC):
                t = TILE["mgate", m]
                bk = 2 * (m % 2)
                if m >= 2:
                    pe.wait_ge(m_ready, m - 1)
                two_blocks(bk, t)
                arrived(t + 1)
                proj_T(bk + 1, 0, t + 1, 0, oA)
                if m == 0:
                    pe.wait_ge(oB_ready, LH)
                proj_T(bk + 1, T, t + 1, 1, oB).then_inc(tile_done, 1)

            def project_out(a, i):
                t = TILE["out", i]
                for k2 in range(2):
                    k = 2 * i + k2
                    for n2 in range(2):
                        o = k2 * D + n2 * 512
                        last = nc.tensor.matmul(PSB[2 * a + n2][:, :], merged[:, k, a * P:(a + 1) * P],
                                                ring[:, slot_of(t), o:o + 512], start=(k == 0), stop=(k == KC - 1))
                return last

            def logits(a):
                pe.wait_ge(hT_ready, 2 * (TA + a + 1))
                for k in range(KC):
                    last = nc.tensor.matmul(PSB[6 + a][:, 0:NE], hT[:, k, a * P:(a + 1) * P], wr[:, k, :],
                                            start=(k == 0), stop=(k == KC - 1))
                last.then_inc(lg_done, 1)

            pe.wait_ge(m_ready, KC)
            for i in range(OUT_TILES):
                arrived(TILE["out", i])
                last = project_out(0, i)
            last.then_inc(yo_done, 1)
            pe.wait_ge(late_in, 80)
            project_out(1, 0).then_inc(tile_done, 1)
            project_out(1, 1).then_inc(tile_done, 1)
            pe.wait_ge(xn_ready, TA + 1)
            transposes(0, 4)
            project_out(1, 2).then_inc(tile_done, 1)
            logits(0)
            project_out(1, 3).then_inc(tile_done, 1)
            pe.wait_ge(xn_ready, TA + 2)
            transposes(1, 4)
            logits(1)
            pe.wait_ge(mask_ready, 2)
            nc.tensor.matmul(PSB[7][:, 0:NE], tri_m, mask[:, 0, :], start=True, stop=True)
            nc.tensor.matmul(PSB[7][:, NE:2 * NE], ones_m, mask[:, 0, :], start=True, stop=False)
            nc.tensor.matmul(PSB[7][:, NE:2 * NE], tri_m, mask[:, 1, :], start=False, stop=True)
            nc.tensor.matmul(PSB[7][:, 2 * NE:3 * NE], ones_m, mask[:, 0, :], start=True, stop=False)
            nc.tensor.matmul(PSB[7][:, 2 * NE:3 * NE], ones_m, mask[:, 1, :], start=False, stop=True).then_inc(rank_done, 1)

            def gather(it):
                pe.wait_ge(sel_ready, it + 1)
                for k in range(KC):
                    for a in range(TA):
                        last = nc.tensor.matmul(PSB[7][:, k * SLOTS:(k + 1) * SLOTS], xn[:, a, k * P:(k + 1) * P],
                                                sel[:, a, :], start=(a == 0), stop=(a == TA - 1))
                last.then_inc(gath_done, 1)

            def scatter(last_one=False):
                for a in range(TA):
                    for n2 in range(2):
                        r = n2 * SLOTS
                        last = nc.tensor.matmul(PSB[2 * a + n2][:, :], gT[r:r + SLOTS, a * P:(a + 1) * P],
                                                ysb[r:r + SLOTS, :], start=False, stop=False, skip_group_check=True)
                    if last_one:
                        last.then_inc(moe_done, 1)
                return last

            def expert(it):
                first = it * E_TILES + (MIX_TILES + 1)
                pe.wait_ge(xs_ready, it + 1)
                pe.wait_ge(oh_ready, it + 1)
                pe.wait_ge(actT_ready, it + 1)
                for g in range(2):
                    for h in range(2):
                        nc.tensor.matmul(PSB[4 + g][h * SLOTS:(h + 1) * SLOTS, :], oh[:, :],
                                         bgu[:, g * D + h * 512:g * D + (h + 1) * 512], start=True, stop=False)
                for k in range(KC):
                    pe.wait_ge(full[k], it * 16 + 16 * (MIX_TILES // RING + 1))
                    for g in range(2):
                        for h in range(2):
                            o = g * D + h * 512
                            last = nc.tensor.matmul(PSB[4 + g][h * SLOTS:(h + 1) * SLOTS, :], xs[:, k, :],
                                                    ring[:, k, o:o + 512], start=False, stop=(k == KC - 1))
                    last.then_inc(tile_done, 1)
                pe.wait_ge(y_ready, it + 1)
                pe.wait_ge(gT_ready, it + 1)
                scatter().then_inc(scat_done, 1)
                pe.wait_ge(gsel_ready, it + 2)
                for a in range(TA):
                    last = nc.tensor.transpose(PSB[6][:, a * P:(a + 1) * P], gsel[:, a, :], ident)
                last.then_inc(gT_done, 1)
                gather(it + 1)
                pe.wait_ge(gT_ready, it + 2)
                pe.wait_ge(act_ready, it + 2)
                for c in range(KC // 2):
                    last = nc.tensor.transpose(PSB[4][:, c * P:(c + 1) * P], ac[:, c * P:(c + 1) * P], ident)
                last.then_inc(actT_done, 1)
                pe.wait_ge(actT_ready, it + 2)
                for i in range(E_TILES - KC):
                    pe.wait_ge(full[KC + i], it * 16 + 16 * (MIX_TILES // RING + 1))
                    for k2 in range(2):
                        k = 2 * i + k2
                        for n2 in range(2):
                            o = k2 * D + n2 * 512
                            last = nc.tensor.matmul(PSB[6][n2 * SLOTS:(n2 + 1) * SLOTS, :],
                                                    acT[:, k % 4, k // 4, :], ring[:, KC + i, o:o + 512],
                                                    start=(k == 0), stop=(k == KC - 1))
                    last.then_inc(tile_done, 1)

            pe.wait_ge(gsel_ready, 1)
            for a in range(TA):
                last = nc.tensor.transpose(PSB[6][:, a * P:(a + 1) * P], gsel[:, a, :], ident)
            last.then_inc(gT_done, 1)
            gather(0)
            with pe.Fori(0, NE) as e:
                expert(e)
            pe.wait_ge(route_ready, 1)
            n = pe.value_load(cnt[0:1, 0:1], min_val=0, max_val=T)
            with pe.If(n > SLOTS):
                with pe.Fori(1, PASSES) as p:
                    with pe.Fori(0, NE) as e:
                        expert(p * NE + e)
                pe.wait_ge(y_ready, PASSES * NE + 1)
                scatter(last_one=True)
            with pe.Else():
                pe.wait_ge(y_ready, NE + 1)
                scatter(last_one=True)

        @block.scalar
        def _(act):
            step = [0]

            def link(ins):
                step[0] += 1
                ins.then_inc(act_step, 1)
                act.wait_ge(act_step, step[0])

            def ln_exp_tables():
                nc.scalar.preload_act_table_set("natural_log_exp_and_others")

            def rstd(src, c, junk):
                link(nc.scalar.activation(junk, src, ACT.Square, accum_out=ss[:, c:c + 1]))
                link(nc.scalar.activation(ss[:, c:c + 1], ss[:, c:c + 1], ACT.Ln, scale=1.0 / D, bias=eps_t[:, :]))
                return nc.scalar.activation(ss[:, c:c + 1], ss[:, c:c + 1], ACT.Exp, scale=-0.5)

            ln_exp_tables()
            act.wait_ge(vec_ready, 1)
            for a in range(TA):
                act.wait_ge(x_in[a], 16)
                rstd(x_t[:, a, :], a, xn[:, a, :]).then_inc(ssq_ready, 1)
            act.wait_ge(vec_ready, 2)
            nc.scalar.activation(dv[:, Y8:Y8 + 8], dv[:, Y8:Y8 + 8], ACT.Exp, scale=-1.0).then_inc(lam_y, 1)
            nc.scalar.activation(dv[:, LBV:LBV + 8], dv[:, LBV:LBV + 8], ACT.Exp, scale=-1.0).then_inc(lam_y, 1)

            S = scr
            for h in range(HEADS + 2):
                p, pp = h - 1, h - 2
                if 0 <= p < HEADS:
                    act.wait_ge(tile_done, 2 * p + 2)
                    if p >= 1:
                        act.wait_ge(gs_ready, p)
                    nc.scalar.activation(S["sigg"][:, :], PSB[3][:, 0:T], ACT.Sigmoid).then_inc(sigg_ready, 1)
                if h < HEADS:
                    act.wait_ge(first_done, 2 * h + 1)
                    if h >= 1:
                        act.wait_ge(qs_ready, h)
                    nc.scalar.activation(S["sigq"][:, :], PSB[0][:, 0:T], ACT.Sigmoid).then_inc(sigq_ready, 1)
                    act.wait_ge(tile_done, 2 * h + 1)
                    if h >= 1:
                        act.wait_ge(f_ready, h)
                    nc.scalar.activation(S["sigf"][:, :], PSB[1][:, 0:T], ACT.Sigmoid).then_inc(sigf_ready, 1)
                ln_exp_tables()
                if h < HEADS:
                    act.wait_ge(f_ready, h + 1)
                    if h >= 1:
                        act.wait_ge(bcum_ready, h)
                    nc.scalar.activation(S["lnf"][:, :], S["f"][:, :], ACT.Ln).then_inc(lnf_ready, 1)
                if pp >= 0:
                    act.wait_ge(ms_done, pp + 1)
                    if pp >= 1:
                        act.wait_ge(oA_ready, pp)
                    link(nc.scalar.activation(S["rinv"][:, :], PSB[6][:, 0:T], ACT.Ln, bias=eps_t[:, :]))
                    nc.scalar.activation(S["rinv"][:, :], S["rinv"][:, :], ACT.Exp, scale=-0.5).then_inc(r_ready, 1)
                if h < HEADS:
                    act.wait_ge(bcum_ready, h + 1)
                    if h >= 1:
                        act.wait_ge(kq_ready, h)
                    nc.scalar.activation(S["eb"][:, :], S["bcum"][:, :], ACT.Exp)
                    nc.scalar.activation(S["enb"][:, :], S["bcum"][:, :], ACT.Exp, scale=-1.0)
                    nc.scalar.activation(S["edec"][:, :], S["dlast"][:, :], ACT.Exp).then_inc(exps_ready, 1)
                    act.wait_ge(first_done, 2 * h + 2)
                    if h >= 2:
                        act.wait_ge(o_done, h - 1)
                    nc.scalar.activation(v_sb[h % 2][:, :, :], PSB[2][:, 0:T].rearrange("p (a n) -> p a n", a=TA),
                                         ACT.Copy).then_inc(v_ready, 1)
                if 0 <= p < HEADS:
                    act.wait_ge(o_done, p + 1)
                    if p >= 1:
                        act.wait_ge(ms_done, p)
                    act.wait_ge(o_copied, p + 1)
                    nc.scalar.activation(S["osq"][:, :], PSB[7][:, 0:T], ACT.Square).then_inc(osq_ready, 1)

            XSQ, ARG, SIG, RS, IG, AD, TH, W = LR

            def copy_branch(n):
                act.wait_ge(tile_done, TILE["xb", n] + 1)
                if n >= 1:
                    act.wait_ge(xc_ready, n)
                nc.scalar.activation(xpad[:, :, CONV - 1:], PSB[4 * (n % 2)][:, :].rearrange("p (b n) -> p b n", b=LB),
                                     ACT.Copy).then_inc(xb_copied, 1)

            copy_branch(0)
            for n in range(LH):
                bk = 4 * (n % 2)
                act.wait_ge(tile_done, TILE["gate", n] + 1)
                if n >= 1:
                    act.wait_ge(oB_ready, n)
                nc.scalar.activation(XSQ[:, :, :], PSB[bk + 1][:, :].rearrange("p (b n) -> p b n", b=LB),
                                     ACT.Square).then_inc(gsq_ready, 1)
                if n + 1 < LH:
                    copy_branch(n + 1)
                act.wait_ge(tile_done, TILE["rg", n] + 1)
                for g, (dst, bc) in enumerate(((RS, C_BA), (IG, C_BX))):
                    for j in range(LB):
                        last = nc.scalar.activation(dst[:, j, :], PSB[bk + 2 + g][:, j * T:(j + 1) * T], ACT.Sigmoid,
                                                    bias=v1(bc + LB * n + j))
                last.then_inc(rsig_ready, 1)
                act.wait_ge(rsig_ready, n + 1)
                for j in range(LB):
                    last = nc.scalar.activation(TH[:, j, :], RS[:, j, :], ACT.Tanh, scale=d1(NC8 + LB * n + j))
                last.then_inc(tanh_ready, 1)
                act.wait_ge(garg_ready, n + 1)
                nc.scalar.activation(SIG[:, :, :], ARG[:, :, :], ACT.Sigmoid, scale=1.5957691216057308).then_inc(gsig_ready, 1)
                ln_exp_tables()
                for j in range(LB):
                    last = nc.scalar.activation(AD[:, j, :], RS[:, j, :], ACT.Exp, scale=d1(C8 + LB * n + j))
                last.then_inc(decay_ready, 1)
                act.wait_ge(th_ready, n + 1)
                nc.scalar.activation(W[:, :, :], TH[:, :, :], ACT.Ln, bias=1.0)
                nc.scalar.activation(TH[:, :, :], TH[:, :, :], ACT.Ln, scale=2.0).then_inc(lns_ready, 1)
                act.wait_ge(w_ready, n + 1)
                nc.scalar.activation(W[:, :, :], W[:, :, :], ACT.Exp, scale=0.5).then_inc(mult_ready, 1)

            for m in range(KC):
                act.wait_ge(tile_done, TILE["mgate", m] + 1)
                if m >= 2:
                    act.wait_ge(m_ready, m - 1)
                nc.scalar.activation(msig[m % 2], PSB[2 * (m % 2)][:, :], ACT.Sigmoid).then_inc(msig_ready, 1)

            ln_exp_tables()
            for a in range(TA):
                act.wait_ge(x1_ready, 2 * a + 2)
                rstd(xn[:, a, :], 2 + a, junk).then_inc(ssq_ready, 1)
                act.wait_ge(negmax_ready, a + 1)
                nc.scalar.activation(e4[:, a, 0:TOPK], top[:, a, 0:TOPK], ACT.Exp, bias=e4[:, a, 4:5],
                                     accum_out=e4[:, a, 5:6]).then_inc(e4_ready, 1)
            act.wait_ge(gT_done, 1)
            nc.scalar.activation(gT[:, :], PSB[6][:, 0:T], ACT.Copy).then_inc(gT_ready, 1)

            def expert(it):
                act.wait_ge(glu_ready, it + 1)
                act.wait_ge(act_ready, it + 1)
                nc.scalar.activation(sg[:, :], glu[:, :], ACT.Sigmoid, scale=ALPHA).then_inc(sig_ready, 1)
                act.wait_ge(gT_done, it + 2)
                nc.scalar.activation(gT[:, :], PSB[6][:, 0:T], ACT.Copy).then_inc(gT_ready, 1)
                act.wait_ge(tile_done, it * E_TILES + (MIX_TILES + E_TILES))
                nc.scalar.activation(ysb[:, :], PSB[6][:, :], ACT.Copy).then_inc(y_ready, 1)

            with act.Fori(0, NE) as e:
                expert(e)
            act.wait_ge(route_ready, 1)
            n = act.value_load(cnt[0:1, 0:1], min_val=0, max_val=T)
            with act.If(n > SLOTS):
                with act.Fori(1, PASSES) as p:
                    with act.Fori(0, NE) as e:
                        expert(p * NE + e)

            ln_exp_tables()
            for a in range(TA):
                act.wait_ge(x2_ready, 2 * a + 2)
                rstd(x_t[:, a, :], 4 + a, xn[:, a, :]).then_inc(frs_ready, 1)

        @block.vector
        def _(dve):
            V = nc.vector
            chain = {"sem": dve_step, "n": 0}

            def link(ins):
                chain["n"] += 1
                ins.then_inc(chain["sem"], 1)
                dve.wait_ge(chain["sem"], chain["n"])

            link(V.memset(eps_t[:, :], EPS))
            link(V.memset(sc_sb[:, :, :], 0.0))
            link(V.memset(gT[:, :], 0.0))
            link(V.memset(xpad[:, :, 0:CONV - 1], 0.0))
            link(V.memset(ranks[:, :, PASSES * NE:], -1.0))
            V.memset(gates[:, :, PASSES * NE:], 0.0).then_inc(vec_ready, 1)
            dve.wait_ge(small_in, 32)
            lam = vec[:, C_LAM:C_LAM + 8]
            c8 = lambda c: dv[:, c:c + 8]
            link(V.tensor_scalar(c8(T0), lam, -1.0, None, ALU.mult))
            link(V.tensor_tensor(c8(Y8), lam, c8(T0), ALU.max))
            V.tensor_tensor(c8(LBV), vec[:, C_LB0:C_LB0 + 8], vec[:, C_LB1:C_LB1 + 8], ALU.subtract).then_inc(vec_ready, 1)

            def normed(src, c, a):
                dve.wait_ge(ssq_ready, c + a + 1)
                V.tensor_scalar(xn[:, a, :], src[:, a, :], ss[:, c + a:c + a + 1], None, ALU.mult).then_inc(xn_ready, 1)

            def fill_hT(a, bank0, c_norm, count):
                for kb in range(2):
                    dve.wait_ge(xT_done, count + kb + 1)
                    w = vec[:, c_norm + 4 * kb:c_norm + 4 * kb + 4].unsqueeze(2).to_broadcast([P, 4, P])
                    V.tensor_tensor(hT[:, 4 * kb:4 * kb + 4, a * P:(a + 1) * P],
                                    PSB[bank0 + kb][:, :].rearrange("p (k t) -> p k t", k=4), w, ALU.mult).then_inc(hT_ready, 1)

            for a in range(TA):
                normed(x_t, 0, a)
            for a in range(TA):
                fill_hT(a, 4 + 2 * a, C_NMIX, 2 * a)
            dve.wait_ge(lam_y, 2)
            link(V.tensor_scalar(c8(LBV), c8(LBV), 1.0, None, ALU.add))
            link(V.reciprocal(c8(LBV), c8(LBV)))
            link(V.tensor_scalar(c8(OML), c8(LBV), -1.0, 1.0, ALU.mult, ALU.add))

            link(V.tensor_scalar(c8(T1), c8(Y8), 2.0, None, ALU.add))
            link(V.reciprocal(c8(T1), c8(T1)))
            link(V.tensor_tensor(c8(T1), c8(Y8), c8(T1), ALU.mult))
            link(V.tensor_tensor(c8(T2), c8(T1), c8(T1), ALU.mult))
            link(V.memset(c8(T3), 1.0 / 17))
            for m in (15, 13, 11, 9, 7, 5, 3, 1):
                link(V.tensor_tensor(c8(T3), c8(T3), c8(T2), ALU.mult))
                link(V.tensor_scalar(c8(T3), c8(T3), 1.0 / m, None, ALU.add))
            link(V.tensor_tensor(c8(T3), c8(T3), c8(T1), ALU.mult))
            link(V.tensor_scalar(c8(T0), c8(T0), 0.0, None, ALU.max))
            link(V.scalar_tensor_tensor(c8(T3), c8(T3), 2.0, c8(T0), ALU.mult, ALU.add))
            link(V.tensor_scalar(c8(NC8), c8(T3), RG_C, None, ALU.mult))
            V.tensor_scalar(c8(C8), c8(T3), -RG_C, None, ALU.mult).then_inc(vec_ready, 1)

            dve.wait_ge(causal_in, 16)
            S = scr
            for h in range(HEADS + 2):
                p, pp = h - 1, h - 2
                if 0 <= p < HEADS:
                    dve.wait_ge(sigg_ready, p + 1)
                    if p >= 2:
                        dve.wait_ge(oA_ready, p - 1)
                    V.tensor_tensor(gs[p % 2][:, :], PSB[3][:, 0:T], S["sigg"][:, :], ALU.mult).then_inc(gs_ready, 1)
                if h < HEADS:
                    dve.wait_ge(sigq_ready, h + 1)
                    if h >= 1:
                        dve.wait_ge(kq_ready, h)
                    V.tensor_tensor(S["qs"][:, :], PSB[0][:, 0:T], S["sigq"][:, :], ALU.mult).then_inc(qs_ready, 1)
                if 0 <= p < HEADS:
                    dve.wait_ge(st1_done, p + 1)
                    if p >= 1:
                        dve.wait_ge(o_done, p)
                    for a in range(TA):
                        V.copy_predicated(sc_sb[:, a, :], causal_m[:, :], PSB[4][:, a * P:(a + 1) * P])
                    V.tensor_copy(kdT[:, :, :], PSB[5][:, 0:T].rearrange("p (a n) -> p a n", a=TA)).then_inc(sc_ready, 1)
                if h < HEADS:
                    dve.wait_ge(sigf_ready, h + 1)
                    if h >= 1:
                        dve.wait_ge(lnf_ready, h)
                    V.tensor_scalar(S["f"][:, :], S["sigf"][:, :], d1(OML + h), d1(LBV + h), ALU.mult, ALU.add).then_inc(f_ready, 1)
                    dve.wait_ge(f_ready, h + 1)
                    V.tensor_scalar(S["k"][:, :], S["f"][:, :], -1.0, 1.0, ALU.mult, ALU.add)
                if 0 <= p < HEADS:
                    dve.wait_ge(st2_done, p + 1)
                    link(V.tensor_copy(S_sb[:, 0, :], PSB[4][:, 0:P]))
                    link(V.scalar_tensor_tensor(S_sb[:, 1, :], S_sb[:, 0, :], decs[p % 2][:, 1:2], PSB[5][:, 0:P], ALU.mult, ALU.add))
                    V.scalar_tensor_tensor(S_sb[:, 2, :], S_sb[:, 1, :], decs[p % 2][:, 2:3], PSB[4][:, P:2 * P],
                                           ALU.mult, ALU.add).then_inc(state_ready, 1)
                if h < HEADS:
                    dve.wait_ge(lnf_ready, h + 1)
                    if h >= 1:
                        dve.wait_ge(exps_ready, h)
                    link(V.tensor_tensor_scan(S["bcum"][:, :], reset_m, S["lnf"][:, :], 0.0, ALU.mult, ALU.add))
                    b3 = S["bcum"][:, :].rearrange("p (n c) -> p n c", c=CH)
                    V.tensor_tensor(S["dlast"][:, :].rearrange("p (n c) -> p n c", c=CH),
                                    b3[:, :, CH - 1:CH].to_broadcast([P, NCH, CH]), b3, ALU.subtract).then_inc(bcum_ready, 1)
                if pp >= 0:
                    dve.wait_ge(r_ready, pp + 1)
                    link(V.tensor_tensor(o_sb[pp % 2][:, :], o_sb[pp % 2][:, :], S["rinv"][:, :], ALU.mult))
                    V.scalar_tensor_tensor(oA[:, pp, :], o_sb[pp % 2][:, :], v1(C_GN + pp), gs[pp % 2][:, :],
                                           ALU.mult, ALU.mult).then_inc(oA_ready, 1)
                if h < HEADS:
                    dve.wait_ge(exps_ready, h + 1)
                if 0 <= p < HEADS:
                    dve.wait_ge(o_done, p + 1)
                    if p >= 2:
                        dve.wait_ge(oA_ready, p - 1)
                    V.tensor_copy(o_sb[p % 2][:, :], PSB[7][:, 0:T]).then_inc(o_copied, 1)
                if h < HEADS:
                    V.tensor_copy(decs[h % 2][:, :], S["eb"][:, CH - 1::CH])
                    V.tensor_tensor(q_in[:, :], S["qs"][:, :], S["eb"][:, :], ALU.mult)
                    V.tensor_tensor(k_in[:, :], S["k"][:, :], S["enb"][:, :], ALU.mult)
                    V.tensor_tensor(k_dec[:, :], S["k"][:, :], S["edec"][:, :], ALU.mult).then_inc(kq_ready, 1)

            XSQ, ARG, SIG, RS, IG, AD, TH, W = LR

            def convolve(n):
                x_c = xc[n % 2]
                dve.wait_ge(xb_copied, n + 1)
                if n >= 2:
                    dve.wait_ge(tile_done, TILE["rg", n - 2] + 1)
                for k in range(CONV):
                    for b in range(LB):
                        c = LB * n + b
                        if k == 0:
                            last = V.tensor_scalar(x_c[:, b, :], xpad[:, b, 0:T], v1(C_CW + c), v1(C_CB + c), ALU.mult, ALU.add)
                        else:
                            last = V.scalar_tensor_tensor(x_c[:, b, :], xpad[:, b, k:k + T], v1(C_CW + 8 * k + c),
                                                          x_c[:, b, :], ALU.mult, ALU.add)
                    if k < CONV - 1:
                        link(last)
                    else:
                        last.then_inc(xc_ready, 1)

            convolve(0)
            for n in range(LH):
                bk = 4 * (n % 2)
                gate_ps = PSB[bk + 1][:, :].rearrange("p (b n) -> p b n", b=LB)
                dve.wait_ge(gsq_ready, n + 1)
                link(V.tensor_scalar(XSQ[:, :, :], XSQ[:, :, :], 0.044715, 1.0, ALU.mult, ALU.add))
                V.tensor_tensor(ARG[:, :, :], gate_ps, XSQ[:, :, :], ALU.mult).then_inc(garg_ready, 1)
                if n + 1 < LH:
                    convolve(n + 1)
                dve.wait_ge(tanh_ready, n + 1)
                V.tensor_scalar(TH[:, :, :], TH[:, :, :], 2.0 ** -64, None, ALU.max).then_inc(th_ready, 1)
                dve.wait_ge(gsig_ready, n + 1)
                link(V.tensor_tensor(SIG[:, :, :], gate_ps, SIG[:, :, :], ALU.mult))
                dve.wait_ge(rsig_ready, n + 1)
                link(V.tensor_tensor(IG[:, :, :], xc[n % 2][:, :, :], IG[:, :, :], ALU.mult))
                dve.wait_ge(lns_ready, n + 1)
                V.tensor_tensor(W[:, :, :], TH[:, :, :], W[:, :, :], ALU.subtract).then_inc(w_ready, 1)
                dve.wait_ge(mult_ready, n + 1)
                link(V.memset(W[:, :, 0:1], 1.0))
                link(V.tensor_tensor(IG[:, :, :], IG[:, :, :], W[:, :, :], ALU.mult))
                dve.wait_ge(decay_ready, n + 1)
                for j in range(LB):
                    last = V.tensor_tensor_scan(ARG[:, j, :], AD[:, j, :], IG[:, j, :], 0.0, ALU.mult, ALU.add)
                link(last)
                V.tensor_tensor(oB[:, LB * n:LB * (n + 1), :], ARG[:, :, :], SIG[:, :, :], ALU.mult).then_inc(oB_ready, 1)

            for m in range(KC):
                dve.wait_ge(msig_ready, m + 1)
                dve.wait_ge(tile_done, TILE["mproj", m] + 1)
                s2 = msig[m % 2]
                link(V.tensor_tensor(s2, PSB[1 + 2 * (m % 2)][:, :], s2, ALU.mult))
                V.tensor_tensor(merged[:, m, :], s2[:, 0:T], s2[:, T:2 * T], ALU.add).then_inc(m_ready, 1)

            V.memset(gsel[:, :, :], 0.0)

            def residual(a):
                dve.wait_ge(*((yo_done, 1) if a == 0 else (tile_done, MIX_TILES)))
                for n2 in range(2):
                    c = slice(n2 * 512, (n2 + 1) * 512)
                    V.tensor_tensor(xn[:, a, c], PSB[2 * a + n2][:, :], x_t[:, a, c], ALU.add).then_inc(x1_ready, 1)
                dve.wait_ge(x1_ready, 2 * a + 2)

            dve.wait_ge(late_in, 80)
            iota_k = iota_m[:, 0:NE].unsqueeze(1).to_broadcast([P, TOPK, NE])

            def choose(a):
                dve.wait_ge(lg_done, a + 1)
                link(V.tensor_tensor(lg[:, a, :], PSB[6 + a][:, 0:NE], br[:, :], ALU.add))
                link(V.max(top[:, a, :], lg[:, a, :]))
                V.tensor_scalar(e4[:, a, 4:5], top[:, a, 0:1], -1.0, None, ALU.mult).then_inc(negmax_ready, 1)
                link(V.max_index(topi[:, a, :], top[:, a, :], lg[:, a, :]))
                link(V.tensor_copy(topf[:, a, :], topi[:, a, :]))
                link(V.tensor_tensor(oneh[:, :, :], iota_k, topf[:, a, 0:TOPK].unsqueeze(2).to_broadcast([P, TOPK, NE]),
                                     ALU.is_equal))
                V.tensor_reduce(mask[:, a, :], oneh[:, :, :].rearrange("p k e -> p e k"), AX.X, ALU.add).then_inc(mask_ready, 1)
                dve.wait_ge(e4_ready, a + 1)
                link(V.reciprocal(e4[:, a, 5:6], e4[:, a, 5:6]))
                link(V.tensor_tensor(oneh[:, :, :], oneh[:, :, :], e4[:, a, 0:TOPK].unsqueeze(2).to_broadcast([P, TOPK, NE]),
                                     ALU.mult))
                link(V.tensor_reduce(gate[:, a, :], oneh[:, :, :].rearrange("p k e -> p e k"), AX.X, ALU.add))
                link(V.tensor_scalar(gates[:, a, 0:NE], gate[:, a, :], e4[:, a, 5:6], None, ALU.mult))
                V.tensor_copy(gsel[:, a, :].rearrange("p (h e) -> p h e", h=2)[:, :, 0:NE],
                              gates[:, a, 0:NE].unsqueeze(1).to_broadcast([P, 2, NE])).then_inc(gated, 1)

            for a in range(TA):
                residual(a)
                normed(xn, 2, a)
                fill_hT(a, 4, C_NFFN, 4 + 2 * a)
                choose(a)
            dve.wait_ge(gated, 2)
            V.tensor_copy(cmax[:, :], e4[:, 0, 5:6]).then_inc(gsel_ready, 1)
            dve.wait_ge(rank_done, 1)
            rank2 = ranks[:, :, 0:NE]
            link(V.scalar_tensor_tensor(rank2, PSB[7][:, 0:TA * NE].rearrange("p (a e) -> p a e", a=TA), 1.0, mask[:, :, :],
                                        ALU.add, ALU.mult))
            link(V.tensor_scalar(rank2, rank2, -1.0, None, ALU.add))
            link(V.reduce_max(cmax[:, :], PSB[7][:, 2 * NE:3 * NE], AX.X))

            STEPS = 2
            nffn_b = vec[:, C_NFFN:C_NFFN + KC].unsqueeze(2).to_broadcast([P, KC, SLOTS])

            def select(it):
                for a in range(TA):
                    last = V.tensor_scalar(sel[:, a, :], iota_m[:, 0:SLOTS], ranks[:, a, bass.ds(it, 1)], None, ALU.is_equal)
                last.then_inc(sel_ready, 1)

            def take_gathered():
                V.tensor_tensor(xs[:, :, :], PSB[7][:, :].rearrange("p (k s) -> p k s", k=KC), nffn_b,
                                ALU.mult).then_inc(xs_ready, 1)

            def expert(it, e):
                chain = [it * STEPS]

                def link(ins):
                    chain[0] = chain[0] + 1
                    ins.then_inc(moe_step, 1)
                    dve.wait_ge(moe_step, chain[0])

                dve.wait_ge(gT_ready, it + 1)
                for a in range(TA):
                    last = V.tensor_scalar(gsel[:, a, :], iota_m, ranks[:, a, bass.ds(it, 1)],
                                           gates[:, a, bass.ds(it, 1)], ALU.is_equal, ALU.mult)
                last.then_inc(gsel_ready, 1)
                dve.wait_ge(xs_ready, it + 1)
                select(it + 1)
                dve.wait_ge(tile_done, it * E_TILES + (MIX_TILES + KC))
                V.tensor_scalar(glu, PSB[4][:, :], LIMIT, None, ALU.min).then_inc(glu_ready, 1)
                link(V.tensor_scalar(lin, PSB[5][:, :], LIMIT, -LIMIT, ALU.min, ALU.max))
                dve.wait_ge(glu_ready, it + 1)
                link(V.scalar_tensor_tensor(lin, lin, 1.0, glu, ALU.add, ALU.mult))
                dve.wait_ge(sig_ready, it + 1)
                V.tensor_tensor(ac, lin, sg, ALU.mult).then_inc(act_ready, 1)
                V.tensor_scalar(oh[:, :], wrap_m[:, bass.ds(e + 1, 1)].to_broadcast([NE, SLOTS]), 1.0, None,
                                ALU.mult).then_inc(oh_ready, 1)
                dve.wait_ge(actT_done, it + 1)
                V.tensor_copy(acT[:, :, :, :].rearrange("p c h s -> p (c h s)"), PSB[4][:, :]).then_inc(actT_ready, 1)
                dve.wait_ge(gath_done, it + 2)
                take_gathered()

            select(0)
            V.tensor_copy(oh[:, :], ident[0:NE, 0:1].to_broadcast([NE, SLOTS])).then_inc(oh_ready, 1)
            V.tensor_copy(e4[:, 0, 7:8], cmax[:, :]).then_inc(actT_ready, 1)
            V.tensor_copy(e4[:, 1, 7:8], cmax[:, :]).then_inc(act_ready, 1)
            V.tensor_copy(e4[:, 1, 6:7], cmax[:, :]).then_inc(y_ready, 1)
            for q in range(1, PASSES):
                V.tensor_scalar(ranks[:, :, q * NE:(q + 1) * NE], rank2, float(-SLOTS * q), None, ALU.add)
                V.tensor_copy(gates[:, :, q * NE:(q + 1) * NE], gates[:, :, 0:NE])
            V.tensor_copy(cnt[:, :], cmax[:, :]).then_inc(route_ready, 1)
            dve.wait_ge(route_ready, 1)
            dve.wait_ge(gath_done, 1)
            take_gathered()
            with dve.Fori(0, NE) as e:
                expert(e, e)
            dve.wait_ge(route_ready, 1)
            n = dve.value_load(cnt[0:1, 0:1], min_val=0, max_val=T)
            with dve.If(n > SLOTS):
                with dve.Fori(1, PASSES) as p:
                    with dve.Fori(0, NE) as e:
                        expert(p * NE + e, e)

            for a in range(TA):
                dve.wait_ge(moe_done, a + 1)
                for n2 in range(2):
                    c = slice(n2 * 512, (n2 + 1) * 512)
                    V.tensor_tensor(x_t[:, a, c], PSB[2 * a + n2][:, :], x_t[:, a, c], ALU.add).then_inc(x2_ready, 1)
            for a in range(TA):
                dve.wait_ge(frs_ready, a + 1)
                V.scalar_tensor_tensor(xn[:, a, :], x_t[:, a, :], ss[:, 4 + a:5 + a], nfin, ALU.mult,
                                       ALU.mult).then_inc(fin_ready, 1)


def constants():
    c = np.zeros((P, K_END), np.float32)
    c[:, K_ID:K_ID + P] = np.eye(P)
    c[:, K_MEAN:K_MEAN + P] = 1.0 / P
    c[:, K_RESET:K_RESET + T] = np.arange(T) % CH != 0
    c[:, K_IOTA:K_IOTA + P] = np.arange(P) % SLOTS
    c[:, K_TRI:K_TRI + P] = np.triu(np.ones((P, P)), 1)
    c[:, K_ONE:K_ONE + P] = 1.0
    c[:NE, K_WRAP:K_WRAP + NE + 1] = np.eye(NE)[:, np.arange(NE + 1) % NE]
    j, i = np.arange(P)[:, None], np.arange(P)[None, :]
    causal = ((i >= j) & (i // CH == j // CH)).astype(np.int32)
    return c, causal


def kernel(**inputs):
    import concourse.bacc as bacc
    from concourse.bass_utils import run_bass_kernel_spmd

    i = {k: np.asarray(v) for k, v in inputs.items()}

    def cols(v):
        return v.reshape(-1, P).T

    vecs = np.concatenate([cols(i[n]) for n in ("norm_mix", "norm_ffn", "gn_w", "conv_w", "conv_b", "b_rg_a", "b_rg_x",
                                                 "lru_lambda", "lb_raw")], axis=1)

    def block(w, c):
        return w[:, c * P:(c + 1) * P].reshape(KC, P, P).transpose(1, 0, 2).reshape(P, D)

    w_in = i["w_in"][0]
    q, f, v, g, xb, gb, ga, gbb = (8 * n for n in range(8))

    def tile(kind, n):
        if kind == "qf":
            return block(w_in, q + n), block(w_in, f + n)
        if kind == "vg":
            return block(w_in, v + n), block(w_in, g + n)
        if kind in ("xb", "gate"):
            c = (xb if kind == "xb" else gb) + LB * n
            return block(w_in, c), block(w_in, c + 1)
        if kind == "rg":
            rg = [i[w][0, n].reshape(LB, P, LB * P).transpose(1, 0, 2).reshape(P, 512) for w in ("w_rg_a", "w_rg_x")]
            return (*rg, np.zeros((P, D), np.float32))
        if kind == "mgate":
            return block(w_in, ga + n), block(w_in, gbb + n)
        if kind == "mproj":
            return block(i["w_proj_a"][0], n), block(i["w_proj_b"][0], n)
        w = i["w_out"][0]
        return w[2 * n * P:(2 * n + 1) * P], w[(2 * n + 1) * P:(2 * n + 2) * P]

    tiles = [tile(*name) for name in ORDER]
    mixw = np.stack([np.concatenate(t, axis=1) for t in tiles])

    w_gu = i["w_gu"][0].reshape(NE, KC, P, D, 2).transpose(0, 1, 2, 4, 3).reshape(NE, KC, P, 2 * D)
    b_gu = i["b_gu"][0].reshape(NE, D, 2).transpose(0, 2, 1).reshape(NE, 2 * D)
    b_down = np.zeros((2, SLOTS, 512), np.float32)
    b_down[:, :NE] = i["b_down"][0].reshape(NE, 2, 512).transpose(1, 0, 2)
    b_down = b_down.reshape(P, 512)
    consts, causal = constants()
    arrays = {
        "x": i["x"][0].reshape(TA, P, D).transpose(1, 0, 2),
        "vecs": vecs, "consts": consts, "causal": causal, "mixw": mixw,
        "w_router": i["w_router"][0].reshape(KC, P, NE).transpose(1, 0, 2),
        "b_router": np.tile(i["b_router"], (P, 1)),
        "w_gu": w_gu, "b_gu": b_gu, "w_down": i["w_down"][0], "b_down": b_down,
        "norm_final": np.tile(i["norm_final"][None], (P, 1)),
    }
    arrays = {f"in_{k}": np.ascontiguousarray(a) for k, a in arrays.items()}
    nc = bacc.Bacc("TRN2", target_bir_lowering=False, num_devices=1)
    args = [nc.dram_tensor(k, a.shape, mybir.dt.from_np(a.dtype), kind="ExternalInput").ap() for k, a in arrays.items()]
    args.append(nc.dram_tensor("out_y", (T, D), mybir.dt.float32, kind="ExternalOutput").ap())
    build(nc, *args)
    r = run_bass_kernel_spmd(nc, [arrays], core_ids=[0])
    return r.results[0]["out_y"].reshape(1, T, D)
```

```python
from contextlib import ExitStack

import numpy as np

import concourse.bass as bass
from concourse import mybir

P = 128
D = 1024
T = 256
TA = T // P
KC = D // P
HEADS = 8
CH = 64
NCH = T // CH
LH = 4
LB = 2
NE = 32
TOPK = 4
SLOTS = 64
PASSES = T // SLOTS
LIMIT = 7.0
ALPHA = 1.702
EPS = 1e-5
CONV = 4
RG_C = 8.0

RING = 12
MIX_RING = 8
TILE_F = 2048
E_TILES = 12
HG_TILES = 2 * HEADS
LRU_TILES = 3 * LH
MERGE_TILES = 2 * KC
OUT_TILES = 4
MIX_TILES = HG_TILES + LRU_TILES + MERGE_TILES + OUT_TILES
assert MIX_TILES % MIX_RING == 0 and E_TILES == RING

C_NMIX, C_NFFN, C_GN, C_CW, C_CB, C_BA, C_BX, C_LAM, C_LB0, C_LB1 = (8 * i for i in (0, 1, 2, 3, 7, 8, 9, 10, 11, 12))
N_VEC = 104
K_ID, K_MEAN, K_RESET, K_IOTA, K_TRI, K_ONE, K_END = 0, 128, 256, 512, 640, 768, 896


ORDER = []
for _n in range(HEADS // 2):
    ORDER += [("qf", 2 * _n), ("vv", _n), ("qf", 2 * _n + 1), ("gg", _n)]
ORDER += [("xb", 0), ("gate", 0)]
for _n in range(LH):
    ORDER += [("xb", _n + 1)] * (_n + 1 < LH) + [("rg", _n)] + [("gate", _n + 1)] * (_n + 1 < LH)
ORDER += [("mgate", 0), ("mgate", 1)]
for _n in range(KC):
    ORDER += [("mgate", _n + 2)] * (_n + 2 < KC) + [("mproj", _n)]
ORDER += [("out", _n) for _n in range(OUT_TILES)]
assert len(ORDER) == MIX_TILES
TILE = {name: t for t, name in enumerate(ORDER)}

SPLIT = [(t, b) for t, (kind, _) in enumerate(ORDER) for b in range(2)
         if kind not in ("rg", "out")]
SPLIT_OF = {tb: m for m, tb in enumerate(SPLIT)}
SPLIT_BUFS = 4


def build(nc, x, vecs, consts, causal, mixw, w_router, b_router, w_gu, b_gu, w_down, b_down, norm_final, out):
    f32 = mybir.dt.float32
    f32r = mybir.dt.float32r
    i32 = mybir.dt.int32
    u32 = mybir.dt.uint32
    ALU = mybir.AluOpType
    ACT = mybir.ActivationFunctionType
    AX = mybir.AxisListType

    ctx = ExitStack()
    with ctx:
        start = {}

        def sb(name, shape, dt=f32):
            buf = ctx.enter_context(nc.sbuf_tensor(name, shape, dt))
            start[name] = nc.sbuf_base - 4 * int(np.prod(shape[1:]))
            return buf

        def over(name, shape, under, offset=0):
            return nc.alloc_sbuf_tensor_at(name, shape, f32r, offset=start[under] + offset)

        def sem(name):
            return ctx.enter_context(nc.semaphore(name))

        ring = sb("ring", [P, RING, TILE_F])
        cst = sb("cst", [P, K_END])
        causal_m = sb("causal_m", [P, P], i32)
        vec = sb("vec", [P, N_VEC])
        eps_t = sb("eps_t", [P, 1])
        ident = cst[:, K_ID:K_ID + P]
        mean_m = cst[:, K_MEAN:K_MEAN + P]
        reset_m = cst[:, K_RESET:K_RESET + T]
        iota_m = cst[:, K_IOTA:K_IOTA + P]
        tri_m = cst[:, K_TRI:K_TRI + P]
        ones_m = cst[:, K_ONE:K_ONE + P]

        x_t = sb("x_t", [P, TA, D])
        xn = sb("xn", [P, TA, D])
        hT = sb("hT", [P, KC, T])
        oA = sb("oA", [P, KC, T])
        oB = sb("oB", [P, KC, T])
        hT_s = (over("hT_hi", [P, KC, T], "hT"), sb("hT_lo", [P, KC, T], f32r))
        oA_s = (over("oA_hi", [P, KC, T], "oA"), over("oA_lo", [P, KC, T], "xn"))
        oB_s = (over("oB_hi", [P, KC, T], "oB"), over("oB_lo", [P, KC, T], "x_t"))
        hT_f = x_t[:, :, :].rearrange("p a (k t) -> p (a k) t", t=T)
        w_s = [over(f"w_{part}", [P, SPLIT_BUFS, D], "ring", 4 * (MIX_RING * TILE_F + i * SPLIT_BUFS * D))
               for i, part in enumerate(("hi", "lo"))]

        def split_buf(part, m):
            return w_s[part][:, m % SPLIT_BUFS, :]

        ss = sb("ss", [P, 8])

        PSB = [ctx.enter_context(nc.psum_tensor(f"psb{i}", [P, 512], f32)) for i in range(8)]

        full = [sem(f"ring_full{i}") for i in range(RING)]
        tile_done = sem("tile_done")
        x_in = [sem(f"x_in{a}") for a in range(TA)]
        ident_in, vec_in = sem("ident_in"), sem("vec_in")
        consts_in = sem("consts_in")
        causal_in = sem("causal_in")
        router_in = sem("router_in")
        x_again = sem("x_again")
        moe_in = sem("moe_in")
        hi_ready = sem("hi_ready")
        lo_ready = sem("lo_ready")
        out_done = sem("out_done")

        def slot_of(t):
            return t % MIX_RING

        act_step = sem("act_step")
        dve_step = sem("dve_step")
        ssq_ready = sem("ssq_ready")
        xn_ready = sem("xn_ready")
        xT_done = sem("xT_done")
        hT_ready = sem("hT_ready")
        hT_hi_ready, hT_lo_ready = sem("hT_hi_ready"), sem("hT_lo_ready")
        vec_ready = sem("vec_ready")
        lam_y = sem("lam_y")
        q_done = sem("q_done")
        sigq_ready, sigf_ready, sigg_ready = sem("sigq_ready"), sem("sigf_ready"), sem("sigg_ready")
        qs_ready = sem("qs_ready")
        f_ready = sem("f_ready")
        lnf_ready = sem("lnf_ready")
        bcum_ready = sem("bcum_ready")
        exps_ready = sem("exps_ready")
        kq_ready = sem("kq_ready")
        v_ready = sem("v_ready")
        gs_ready = sem("gs_ready")
        st1_done = sem("st1_done")
        sc_ready = sem("sc_ready")
        st2_done = sem("st2_done")
        state_ready = sem("state_ready")
        o_done = sem("o_done")
        osq_ready = sem("osq_ready")
        o_copied = sem("o_copied")
        ms_done = sem("ms_done")
        r_ready = sem("r_ready")
        oA_ready = sem("oA_ready")
        xb_copied = sem("xb_copied")
        xc_ready = sem("xc_ready")
        rsig_ready = sem("rsig_ready")
        tanh_ready = sem("tanh_ready")
        th_ready, lns_ready = sem("th_ready"), sem("lns_ready")
        w_ready = sem("w_ready")
        decay_ready = sem("decay_ready")
        mult_ready = sem("mult_ready")
        gsq_ready = sem("gsq_ready")
        garg_ready = sem("garg_ready")
        gsig_ready = sem("gsig_ready")
        oB_ready = sem("oB_ready")
        msig_ready = sem("msig_ready")
        m_ready = sem("m_ready")
        x1_ready = sem("x1_ready")
        yo_done = sem("yo_done")
        gated = sem("gated")
        lg_done = sem("lg_done")
        negmax_ready = sem("negmax_ready")
        e4_ready = sem("e4_ready")
        mask_ready = sem("mask_ready")
        rank_done = sem("rank_done")
        count_done, count_read = sem("count_done"), sem("count_read")
        route_ready = sem("route_ready")
        sel_ready = sem("sel_ready")
        gath_done = sem("gath_done")
        xs_ready = sem("xs_ready")
        moe_step = sem("moe_step")
        glu_ready = sem("glu_ready")
        sig_ready = sem("sig_ready")
        act_ready = sem("act_ready")
        oh_ready = sem("oh_ready")
        actT_done = sem("actT_done")
        actT_ready = sem("actT_ready")
        gsel_ready = sem("gsel_ready")
        gT_done = sem("gT_done")
        gT_ready = sem("gT_ready")
        y_ready = sem("y_ready")
        moe_done = sem("moe_done")
        x2_ready = sem("x2_ready")
        frs_ready = sem("frs_ready")
        fin_ready = sem("fin_ready")

        scr = {}
        names = ("sigq", "sigf", "qs", "f", "k", "lnf", "bcum", "dlast", "eb", "enb", "edec", "osq", "rinv")
        hg = sb("hg", [P, len(names), T])
        for i, n in enumerate(names):
            scr[n] = hg[:, i, :]
        msig = [hg[:, i:i + 2, :].rearrange("p a t -> p (a t)") for i in (0, 2, 10)]
        q_in, k_in, k_dec = sb("q_in", [P, T]), sb("k_in", [P, T]), sb("k_dec", [P, T])
        gs = sb("gs", [P, 2 * T])
        o_sb = [sb(f"o_sb{i}", [P, T]) for i in range(2)]
        v_sb = sb("v_sb", [P, TA, 2 * P])
        decs = [sb(f"decs{i}", [P, NCH]) for i in range(2)]
        kdT = sb("kdT", [P, TA, P])
        sc_sb = sb("sc_sb", [P, TA, P])
        S_sb = sb("S_sb", [P, NCH - 1, P])
        dv = sb("dv", [P, 96])
        LBV, OML, C8, NC8, Y8, T0, T1, T2, T3 = (8 * i for i in range(9))
        xpad = sb("xpad", [P, LB, T + CONV - 1])
        xc = [sb(f"xc{i}", [P, LB, T]) for i in range(2)]
        lr = sb("lr", [P, 8, LB, T])
        LR = [lr[:, i, :, :] for i in range(8)]
        merged = lr[:, 0:4, :, :].rearrange("p i b t -> p (i b) t")
        wr = sb("wr", [P, KC, NE])
        br = sb("br", [P, NE])
        nfin = oA[:, 4:8, :].rearrange("p k t -> p (k t)")
        bgu = oB[0:NE, :, :].rearrange("p k t -> p (k t)")
        oh = sb("oh", [NE, SLOTS])
        lg = sb("lg", [P, TA, NE])
        top = sb("top", [P, TA, 8])
        topi = sb("topi", [P, TA, 8], u32)
        topf = sb("topf", [P, TA, 8])
        e4 = sb("e4", [P, TA, 8])
        oneh = sb("oneh", [P, TOPK, NE])
        gate = sb("gate", [P, TA, NE])
        gates = sb("gates", [P, TA, PASSES * NE])
        mask = sb("mask", [P, TA, NE])
        ranks = sb("ranks", [P, TA, PASSES * NE])
        cmax = sb("cmax", [P, 1])
        cnt = sb("cnt", [P, 1], i32)
        sel = sb("sel", [P, TA, SLOTS])
        gsel = sb("gsel", [P, TA, P])
        junk = hg[:, 4:8, :].rearrange("p a t -> p (a t)")
        xs = LR[4][:, :, :].rearrange("p b n -> p (b n)").rearrange("p (k s) -> p k s", k=KC)
        glu = LR[0][:, :, :].rearrange("p b n -> p (b n)")
        lin = LR[1][:, :, :].rearrange("p b n -> p (b n)")
        sg = LR[5][:, :, :].rearrange("p b n -> p (b n)")
        acT = LR[6][:, :, :].rearrange("p b n -> p (b n)").rearrange("p (c h s) -> p c h s", c=KC // 2, h=2)
        ac = LR[2][:, :, :].rearrange("p b n -> p (b n)")
        gT = sb("gT", [P, T])
        ysb = hg[:, 8:10, :].rearrange("p a t -> p (a t)")

        def v1(c):
            return vec[:, c:c + 1]

        def d1(c):
            return dv[:, c:c + 1]

        block = ctx.enter_context(nc.Block())

        @block.sync
        def _(sp):
            for a in range(TA):
                sp.dma_start(x_t[:, a, :], x[:, a, :]).then_inc(x_in[a], 16)
            sp.dma_start(ident, consts[:, K_ID:K_ID + P]).then_inc(ident_in, 16)
            sp.dma_start(vec[:, :], vecs).then_inc(vec_in, 16)
            for t in range(MIX_TILES):
                if t == 1:
                    sp.dma_start(cst[:, P:], consts[:, P:]).then_inc(consts_in, 16)
                if t >= MIX_RING:
                    sp.wait_ge(tile_done, t - MIX_RING + 1)
                sp.dma_start(ring[:, slot_of(t), :], mixw[t]).then_inc(full[slot_of(t)], 16)

            def load_tile(e, i):
                src = (w_gu[e, i] if i < KC else
                       w_down[e, 2 * P * (i - KC):2 * P * (i - KC + 1), :].rearrange("(b p) n -> p b n", p=P))
                dst = ring[:, i, :] if i < KC else ring[:, i, :].rearrange("p (b n) -> p b n", b=2)
                sp.dma_start(dst, src).then_inc(full[i], 16)

            def load_expert(it, e):
                for i in range(E_TILES):
                    sp.wait_ge(tile_done, it * E_TILES + (MIX_TILES - E_TILES + i + 1))
                    load_tile(e, i)

            sp.wait_ge(tile_done, MIX_TILES - OUT_TILES)
            for a in range(TA):
                sp.dma_start(x_t[:, a, :], x[:, a, :]).then_inc(x_again, 16)
            sp.dma_start(ysb, b_down).then_inc(y_ready, 16)
            sp.dma_start(nfin, norm_final).then_inc(moe_in, 16)
            sp.dma_start(bgu, b_gu).then_inc(moe_in, 16)
            for i in range(E_TILES):
                if i < MIX_RING:
                    sp.wait_ge(tile_done, MIX_TILES - MIX_RING + i + 1)
                load_tile(0, i)
            with sp.Fori(1, NE) as e:
                load_expert(e, e)
            sp.wait_ge(route_ready, 1)
            n = sp.value_load(cnt[0:1, 0:1], min_val=0, max_val=T)
            with sp.If(n > SLOTS):
                with sp.Fori(1, PASSES) as p:
                    with sp.Fori(0, NE) as e:
                        load_expert(p * NE + e, e)
            for a in range(TA):
                sp.wait_ge(fin_ready, a + 1)
                sp.dma_start(out[a * P:(a + 1) * P, :], xn[:, a, :]).then_inc(out_done, 16)
            sp.wait_ge(out_done, 16 * TA)

        @block.gpsimd
        def _(pool):
            pool.dma_start(causal_m[:, :], causal).then_inc(causal_in, 16)
            pool.dma_start(wr[:, :, :], w_router).then_inc(router_in, 16)
            pool.dma_start(br[:, :], b_router).then_inc(router_in, 16)
            for m, (t, b) in enumerate(SPLIT):
                pool.wait_ge(hi_ready, m + 1)
                nc.gpsimd.tensor_tensor(split_buf(1, m), ring[:, slot_of(t), b * D:(b + 1) * D],
                                        split_buf(0, m).bitcast(f32), ALU.subtract).then_inc(lo_ready, 1)

        @block.tensor
        def _(pe):
            def arrived(t):
                pe.wait_ge(full[slot_of(t)], 16 * (t // MIX_RING + 1))

            def wblk(t, b, k):
                o = b * D + k * P
                return ring[:, slot_of(t), o:o + P]

            def transposes(a, kb, bank):
                for k4 in range(4):
                    k = 4 * kb + k4
                    last = nc.tensor.transpose(PSB[bank][:, k4 * P:(k4 + 1) * P], xn[:, a, k * P:(k + 1) * P], ident)
                last.then_inc(xT_done, 1)

            pe.wait_ge(ident_in, 16)
            for kb in range(2):
                for a in range(TA):
                    pe.wait_ge(xn_ready, a + 1)
                    transposes(a, kb, 4 + 2 * a + kb)
            pe.wait_ge(consts_in, 16)

            def proj_T(bank, col, t, b, rhs):
                m = SPLIT_OF[t, b]
                pe.wait_ge(hi_ready, m + 1)
                for k in range(KC):
                    if m == 0:
                        pe.wait_ge(hT_lo_ready, 2 + 2 * (k // 4))
                    for xp in range(2):
                        nc.tensor.matmul(PSB[bank][:, col:col + T], split_buf(0, m)[:, k * P:(k + 1) * P], rhs[xp][:, k, :],
                                         start=(k == 0 and xp == 0), stop=False)
                pe.wait_ge(lo_ready, m + 1)
                for k in range(KC):
                    last = nc.tensor.matmul(PSB[bank][:, col:col + T], split_buf(1, m)[:, k * P:(k + 1) * P], rhs[0][:, k, :],
                                            start=False, stop=(k == KC - 1))
                return last

            def proj_v(j, b):
                m = SPLIT_OF[TILE["vv", j], b]
                pe.wait_ge(hi_ready, m + 1)
                for wp, xps in ((0, (0, 1)), (1, (0,))):
                    if wp == 1:
                        pe.wait_ge(lo_ready, m + 1)
                    for a in range(TA):
                        for k4 in range(KC // 2):
                            for xp in xps:
                                last = nc.tensor.matmul(PSB[2][:, a * 2 * P:(a + 1) * 2 * P],
                                                        hT_s[xp][:, 4 * b + k4, a * P:(a + 1) * P],
                                                        split_buf(wp, m)[:, k4 * 2 * P:(k4 + 1) * 2 * P],
                                                        start=(b == 0 and wp == 0 and a == 0 and k4 == 0 and xp == 0),
                                                        stop=(b == 1 and wp == 1 and k4 == 3), skip_group_check=True)
                return last

            for h in range(HEADS + 1):
                p = h - 1
                vc = slice((p % 2) * P, (p % 2 + 1) * P)
                if h < HEADS:
                    if h >= 1:
                        pe.wait_ge(qs_ready, h)
                    proj_T(0, 0, 2 * h, 0, hT_s).then_inc(q_done, 1)
                else:
                    pe.wait_ge(qs_ready, HEADS)
                    proj_T(0, 0, TILE["xb", 0], 0, hT_s)
                if p >= 0:
                    pe.wait_ge(kq_ready, p + 1)
                    if p >= 1:
                        pe.wait_ge(state_ready, p)
                    for a in range(TA):
                        nc.tensor.matmul(PSB[4][:, a * P:(a + 1) * P], k_in[:, a * P:(a + 1) * P],
                                         q_in[:, a * P:(a + 1) * P], start=True, stop=True)
                    for a in range(TA):
                        last = nc.tensor.transpose(PSB[5][:, a * P:(a + 1) * P], k_dec[:, a * P:(a + 1) * P], ident)
                    last.then_inc(st1_done, 1)
                if h < HEADS:
                    if h >= 1:
                        pe.wait_ge(sigf_ready, h)
                    proj_T(1, 0, 2 * h, 1, hT_s).then_inc(tile_done, 1)
                else:
                    proj_T(0, T, TILE["xb", 0], 1, hT_s).then_inc(tile_done, 1)
                if p >= 0:
                    pe.wait_ge(sc_ready, p + 1)
                    pe.wait_ge(v_ready, p // 2 + 1)
                    for n in range(NCH - 1):
                        a, r = n // 2, CH * (n % 2)
                        bank, col = (4, a * P) if n % 2 == 0 else (5, 0)
                        last = nc.tensor.matmul(PSB[bank][:, col:col + P], kdT[r:r + CH, a, :],
                                                v_sb[r:r + CH, a, vc], start=True, stop=True)
                    last.then_inc(st2_done, 1)
                if h < HEADS and h % 2 == 0:
                    if h >= 2:
                        pe.wait_ge(v_ready, h // 2)
                    proj_v(h // 2, 0)
                elif h < HEADS:
                    if h >= 2:
                        pe.wait_ge(gs_ready, h // 2)
                    proj_T(3, 0, TILE["gg", h // 2], 0, hT_s)
                else:
                    pe.wait_ge(sigf_ready, HEADS)
                    proj_T(1, 0, TILE["gate", 0], 0, hT_s)
                if p >= 0:
                    pe.wait_ge(state_ready, p + 1)
                    if p >= 1:
                        pe.wait_ge(osq_ready, p)
                        pe.wait_ge(o_copied, p)
                    for a in range(TA):
                        nc.tensor.matmul(PSB[7][:, a * P:(a + 1) * P], v_sb[:, a, vc], sc_sb[:, a, :],
                                         start=True, stop=False)
                        for n in (2 * a, 2 * a + 1):
                            if n:
                                last = nc.tensor.matmul(PSB[7][:, n * CH:(n + 1) * CH], S_sb[:, n - 1, :],
                                                        q_in[:, n * CH:(n + 1) * CH], start=False, stop=(n % 2 == 1))
                    last.then_inc(o_done, 1)
                if h < HEADS and h % 2 == 0:
                    proj_v(h // 2, 1).then_inc(tile_done, 1)
                elif h < HEADS:
                    proj_T(3, T, TILE["gg", h // 2], 1, hT_s).then_inc(tile_done, 1)
                else:
                    proj_T(1, T, TILE["gate", 0], 1, hT_s).then_inc(tile_done, 1)
                if p >= 0:
                    pe.wait_ge(osq_ready, p + 1)
                    if p >= 1:
                        pe.wait_ge(r_ready, p)
                    nc.tensor.matmul(PSB[6][:, 0:T], mean_m, scr["osq"][:, :], start=True, stop=True).then_inc(ms_done, 1)

            def two_blocks(bank, t):
                arrived(t)
                proj_T(bank, 0, t, 0, hT_s)
                proj_T(bank, T, t, 1, hT_s).then_inc(tile_done, 1)

            for n in range(LH):
                bk, nbk = 4 * (n % 2), 4 * ((n + 1) % 2)
                if n + 1 < LH:
                    if n == 0:
                        pe.wait_ge(state_ready, HEADS)
                        pe.wait_ge(o_copied, HEADS)
                    else:
                        pe.wait_ge(xb_copied, n)
                    two_blocks(nbk, TILE["xb", n + 1])
                t = TILE["rg", n]
                arrived(t)
                pe.wait_ge(xc_ready, n + 1)
                if n == 0:
                    pe.wait_ge(gs_ready, HEADS // 2)
                    pe.wait_ge(v_ready, HEADS // 2)
                elif n == 1:
                    pe.wait_ge(r_ready, HEADS)
                    pe.wait_ge(osq_ready, HEADS)
                else:
                    pe.wait_ge(rsig_ready, n - 1)
                for g in range(2):
                    for j in range(LB):
                        for i in range(LB):
                            o = g * 512 + i * T + j * P
                            last = nc.tensor.matmul(PSB[bk + 2 + g][:, j * T:(j + 1) * T], ring[:, slot_of(t), o:o + P],
                                                    xc[n % 2][:, i, :], start=(i == 0), stop=(i == LB - 1))
                last.then_inc(tile_done, 1)
                if n + 1 < LH:
                    if n >= 1:
                        pe.wait_ge(oB_ready, n)
                    two_blocks(nbk + 1, TILE["gate", n + 1])


            def merge_gates(m):
                if m >= 4:
                    pe.wait_ge(m_ready, m - 3)
                two_blocks(2 * (m % 4), TILE["mgate", m])

            pe.wait_ge(xb_copied, LH - 1)
            merge_gates(0)
            pe.wait_ge(rsig_ready, LH - 1)
            merge_gates(1)
            pe.wait_ge(oA_ready, HEADS)
            pe.wait_ge(oB_ready, LH - 1)
            pe.wait_ge(xb_copied, LH)
            for m in range(KC):
                if m + 2 < KC:
                    if m == 1:
                        pe.wait_ge(rsig_ready, LH)
                    merge_gates(m + 2)
                t = TILE["mproj", m]
                arrived(t)
                proj_T(2 * (m % 4) + 1, 0, t, 0, oA_s)
                if m == 0:
                    pe.wait_ge(oB_ready, LH)
                proj_T(2 * (m % 4) + 1, T, t, 1, oB_s).then_inc(tile_done, 1)

            def project_out(a, i):
                t = TILE["out", i]
                for k2 in range(2):
                    k = 2 * i + k2
                    for n2 in range(2):
                        o = k2 * D + n2 * 512
                        last = nc.tensor.matmul(PSB[2 * a + n2][:, :], merged[:, k, a * P:(a + 1) * P],
                                                ring[:, slot_of(t), o:o + 512], start=(k == 0), stop=(k == KC - 1))
                return last

            def logits(a):
                for k in range(KC):
                    if k % 4 == 0:
                        pe.wait_ge(hT_ready, 2 * (TA + a) + k // 4 + 1)
                    last = nc.tensor.matmul(PSB[7 - a][:, 0:NE], hT[:, k, a * P:(a + 1) * P], wr[:, k, :],
                                            start=(k == 0), stop=(k == KC - 1))
                last.then_inc(lg_done, 1)

            for i in range(OUT_TILES):
                pe.wait_ge(m_ready, max(KC - 2, 2 * i + 2))
                arrived(TILE["out", i])
                last = project_out(0, i)
            last.then_inc(yo_done, 1)
            pe.wait_ge(router_in, 32)
            project_out(1, 0).then_inc(tile_done, 1)
            project_out(1, 1).then_inc(tile_done, 1)
            for kb in range(2):
                pe.wait_ge(x1_ready, kb + 1)
                transposes(0, kb, 4 + kb)
            project_out(1, 2).then_inc(tile_done, 1)
            logits(0)
            project_out(1, 3).then_inc(tile_done, 1)
            pe.wait_ge(mask_ready, 1)
            for kb in range(2):
                pe.wait_ge(x1_ready, TA + kb + 1)
                transposes(1, kb, 6 + kb)
            logits(1)
            pe.wait_ge(hT_ready, 2 * (TA + 2))
            nc.tensor.matmul(PSB[7][:, 0:NE], tri_m, mask[:, 0, :], start=True, stop=True)
            nc.tensor.matmul(PSB[7][:, NE:2 * NE], ones_m, mask[:, 0, :], start=True, stop=False)
            pe.wait_ge(mask_ready, 2)
            nc.tensor.matmul(PSB[7][:, NE:2 * NE], tri_m, mask[:, 1, :], start=False, stop=True).then_inc(rank_done, 1)
            nc.tensor.matmul(PSB[6][:, 0:NE], ones_m, mask[:, 0, :], start=True, stop=False)
            nc.tensor.matmul(PSB[6][:, 0:NE], ones_m, mask[:, 1, :], start=False, stop=True).then_inc(count_done, 1)

            def gather(half):
                for k in range(half * KC // 2, (half + 1) * KC // 2):
                    for a in range(TA):
                        last = nc.tensor.matmul(PSB[7][:, k * SLOTS:(k + 1) * SLOTS], xn[:, a, k * P:(k + 1) * P],
                                                sel[:, a, :], start=(a == 0), stop=(a == TA - 1))
                last.then_inc(gath_done, 1)

            def scatter(last_one=False):
                for a in range(TA):
                    for n2 in range(2):
                        r = n2 * SLOTS
                        last = nc.tensor.matmul(PSB[2 * a + n2][:, :], gT[r:r + SLOTS, a * P:(a + 1) * P],
                                                ysb[r:r + SLOTS, :], start=False, stop=False, skip_group_check=True)
                    if last_one:
                        last.then_inc(moe_done, 1)
                return last

            def expert(it):
                pe.wait_ge(sel_ready, it + 1)
                gather(0)
                pe.wait_ge(xs_ready, 2 * it + 1)
                for k in range(KC):
                    if k == KC // 2 - 1:
                        gather(1)
                    elif k == KC // 2:
                        pe.wait_ge(xs_ready, 2 * it + 2)
                    elif k == KC - 1:
                        pe.wait_ge(oh_ready, it + 1)
                        for g in range(2):
                            for h in range(2):
                                nc.tensor.matmul(PSB[4 + g][h * SLOTS:(h + 1) * SLOTS, :], oh[:, :],
                                                 bgu[:, g * D + h * 512:g * D + (h + 1) * 512], start=False, stop=False)
                    pe.wait_ge(full[k], it * 16 + 16 * (MIX_TILES // MIX_RING + 1))
                    for g in range(2):
                        for h in range(2):
                            o = g * D + h * 512
                            last = nc.tensor.matmul(PSB[4 + g][h * SLOTS:(h + 1) * SLOTS, :], xs[:, k, :],
                                                    ring[:, k, o:o + 512], start=(k == 0), stop=(k == KC - 1))
                    last.then_inc(tile_done, 1)
                pe.wait_ge(y_ready, it + 16)
                pe.wait_ge(gT_ready, it + 1)
                scatter()
                pe.wait_ge(act_ready, it + 1)
                for c in range(KC // 2):
                    last = nc.tensor.transpose(PSB[4][:, c * P:(c + 1) * P], ac[:, c * P:(c + 1) * P], ident)
                last.then_inc(actT_done, 1)
                pe.wait_ge(gsel_ready, it + 1)
                for a in range(TA):
                    last = nc.tensor.transpose(PSB[6][:, a * P:(a + 1) * P], gsel[:, a, :], ident)
                last.then_inc(gT_done, 1)
                pe.wait_ge(actT_ready, it + 1)
                pe.wait_ge(gT_ready, it + 2)
                for i in range(E_TILES - KC):
                    pe.wait_ge(full[KC + i], it * 16 + 16)
                    for k2 in range(2):
                        k = 2 * i + k2
                        for n2 in range(2):
                            o = k2 * D + n2 * 512
                            last = nc.tensor.matmul(PSB[6][n2 * SLOTS:(n2 + 1) * SLOTS, :],
                                                    acT[:, k % 4, k // 4, :], ring[:, KC + i, o:o + 512],
                                                    start=(k == 0), stop=(k == KC - 1))
                    last.then_inc(tile_done, 1)

            pe.wait_ge(gated, TA)
            for a in range(TA):
                last = nc.tensor.transpose(PSB[4][:, a * P:(a + 1) * P], gsel[:, a, :], ident)
            last.then_inc(gT_done, 1)
            pe.wait_ge(xn_ready, 2 * TA)
            pe.wait_ge(moe_in, 32)
            pe.wait_ge(gT_ready, 1)
            pe.wait_ge(count_read, 1)
            with pe.Fori(0, NE) as e:
                expert(e)
            pe.wait_ge(route_ready, 1)
            n = pe.value_load(cnt[0:1, 0:1], min_val=0, max_val=T)
            with pe.If(n > SLOTS):
                with pe.Fori(1, PASSES) as p:
                    with pe.Fori(0, NE) as e:
                        expert(p * NE + e)
                pe.wait_ge(y_ready, PASSES * NE + 16)
                scatter(last_one=True)
            with pe.Else():
                pe.wait_ge(y_ready, NE + 16)
                scatter(last_one=True)

        @block.scalar
        def _(act):
            step = [0]

            def link(ins):
                step[0] += 1
                ins.then_inc(act_step, 1)
                act.wait_ge(act_step, step[0])

            def ln_exp_tables():
                nc.scalar.preload_act_table_set("natural_log_exp_and_others")

            def rstd(src, c, junk):
                link(nc.scalar.activation(junk, src, ACT.Square, accum_out=ss[:, c:c + 1]))
                link(nc.scalar.activation(ss[:, c:c + 1], ss[:, c:c + 1], ACT.Ln, scale=1.0 / D, bias=eps_t[:, :]))
                return nc.scalar.activation(ss[:, c:c + 1], ss[:, c:c + 1], ACT.Exp, scale=-0.5)

            def split(m):
                if m >= SPLIT_BUFS:
                    t, b = SPLIT[m - SPLIT_BUFS]
                    if ORDER[t][0] == "qf" and b == 0:
                        act.wait_ge(q_done, t // 2 + 1)
                    else:
                        act.wait_ge(tile_done, t + 1)
                t, b = SPLIT[m]
                act.wait_ge(full[slot_of(t)], 16 * (t // MIX_RING + 1))
                nc.scalar.activation(split_buf(0, m), ring[:, slot_of(t), b * D:(b + 1) * D], ACT.Copy).then_inc(hi_ready, 1)

            def split_tile(kind, n):
                for b in range(2):
                    split(SPLIT_OF[TILE[kind, n], b])

            ln_exp_tables()
            act.wait_ge(vec_ready, 1)
            for a in range(TA):
                act.wait_ge(x_in[a], 16)
                rstd(x_t[:, a, :], a, xn[:, a, :]).then_inc(ssq_ready, 1)
            split(0)
            for i in range(4):
                kb, a = i // 2, i % 2
                piece = (slice(None), slice(4 * kb, 4 * kb + 4), slice(a * P, (a + 1) * P))
                act.wait_ge(hT_ready, i + 1)
                nc.scalar.activation(hT_s[0][piece], hT_f[piece], ACT.Copy).then_inc(hT_hi_ready, 1)
            split(1)
            act.wait_ge(vec_ready, 2)
            nc.scalar.activation(dv[:, Y8:Y8 + 8], dv[:, Y8:Y8 + 8], ACT.Exp, scale=-1.0).then_inc(lam_y, 1)
            nc.scalar.activation(dv[:, LBV:LBV + 8], dv[:, LBV:LBV + 8], ACT.Exp, scale=-1.0).then_inc(lam_y, 1)
            split(2)
            split(3)

            S = scr
            for h in range(HEADS + 2):
                p, pp = h - 1, h - 2
                if h % 2 == 0 and 2 <= h <= HEADS:
                    act.wait_ge(tile_done, TILE["gg", h // 2 - 1] + 1)
                    if h >= 4:
                        act.wait_ge(oA_ready, h - 2)
                    nc.scalar.activation(gs[:, :], PSB[3][:, :], ACT.Sigmoid).then_inc(sigg_ready, 1)
                if h < HEADS:
                    act.wait_ge(q_done, h + 1)
                    if h >= 1:
                        act.wait_ge(qs_ready, h)
                    nc.scalar.activation(S["sigq"][:, :], PSB[0][:, 0:T], ACT.Sigmoid).then_inc(sigq_ready, 1)
                    split(SPLIT_OF[2 * h, 0] + SPLIT_BUFS)
                    act.wait_ge(tile_done, 2 * h + 1)
                    if h >= 1:
                        act.wait_ge(f_ready, h)
                    nc.scalar.activation(S["sigf"][:, :], PSB[1][:, 0:T], ACT.Sigmoid).then_inc(sigf_ready, 1)
                    split(SPLIT_OF[2 * h, 1] + SPLIT_BUFS)
                ln_exp_tables()
                if h < HEADS:
                    act.wait_ge(f_ready, h + 1)
                    if h >= 1:
                        act.wait_ge(bcum_ready, h)
                    nc.scalar.activation(S["lnf"][:, :], S["f"][:, :], ACT.Ln).then_inc(lnf_ready, 1)
                if pp >= 0:
                    act.wait_ge(ms_done, pp + 1)
                    if pp >= 1:
                        act.wait_ge(oA_ready, pp)
                    link(nc.scalar.activation(S["rinv"][:, :], PSB[6][:, 0:T], ACT.Ln, bias=eps_t[:, :]))
                    nc.scalar.activation(S["rinv"][:, :], S["rinv"][:, :], ACT.Exp, scale=-0.5).then_inc(r_ready, 1)
                if h < HEADS:
                    act.wait_ge(bcum_ready, h + 1)
                    if h >= 1:
                        act.wait_ge(kq_ready, h)
                    nc.scalar.activation(S["eb"][:, :], S["bcum"][:, :], ACT.Exp)
                    nc.scalar.activation(S["enb"][:, :], S["bcum"][:, :], ACT.Exp, scale=-1.0)
                    nc.scalar.activation(S["edec"][:, :], S["dlast"][:, :], ACT.Exp).then_inc(exps_ready, 1)
                if h == HEADS:
                    split_tile("xb", 1)
                if 0 <= p < HEADS:
                    act.wait_ge(o_done, p + 1)
                    if p >= 1:
                        act.wait_ge(ms_done, p)
                    act.wait_ge(o_copied, p + 1)
                    nc.scalar.activation(S["osq"][:, :], PSB[7][:, 0:T], ACT.Square).then_inc(osq_ready, 1)
                if h < HEADS and h % 2 == 0:
                    act.wait_ge(tile_done, TILE["vv", h // 2] + 1)
                    if h >= 2:
                        act.wait_ge(o_done, h)
                    nc.scalar.activation(v_sb[:, :, :], PSB[2][:, :].rearrange("p (a n) -> p a n", a=TA),
                                         ACT.Copy).then_inc(v_ready, 1)
                if h < HEADS:
                    for b in range(2):
                        split(SPLIT_OF[2 * h + 1, b] + SPLIT_BUFS)

            XSQ, ARG, SIG, RS, IG, AD, TH, W = LR

            def copy_branch(n):
                act.wait_ge(tile_done, TILE["xb", n] + 1)
                if n >= 1:
                    act.wait_ge(xc_ready, n)
                nc.scalar.activation(xpad[:, :, CONV - 1:], PSB[4 * (n % 2)][:, :].rearrange("p (b n) -> p b n", b=LB),
                                     ACT.Copy).then_inc(xb_copied, 1)

            copy_branch(0)
            for n in range(LH):
                bk = 4 * (n % 2)
                act.wait_ge(tile_done, TILE["gate", n] + 1)
                split_tile(*(("gate", n + 1) if n + 1 < LH else ("mgate", 1)))
                if n >= 1:
                    act.wait_ge(garg_ready, n)
                nc.scalar.activation(XSQ[:, :, :], PSB[bk + 1][:, :].rearrange("p (b n) -> p b n", b=LB),
                                     ACT.Square).then_inc(gsq_ready, 1)
                if n + 1 < LH:
                    copy_branch(n + 1)
                    split_tile(*(("xb", n + 2) if n + 2 < LH else ("mgate", 0)))
                act.wait_ge(tile_done, TILE["rg", n] + 1)
                if n >= 1:
                    act.wait_ge(oB_ready, n)
                for g, (dst, bc) in enumerate(((RS, C_BA), (IG, C_BX))):
                    for j in range(LB):
                        last = nc.scalar.activation(dst[:, j, :], PSB[bk + 2 + g][:, j * T:(j + 1) * T], ACT.Sigmoid,
                                                    bias=v1(bc + LB * n + j))
                last.then_inc(rsig_ready, 1)
                act.wait_ge(rsig_ready, n + 1)
                for j in range(LB):
                    last = nc.scalar.activation(TH[:, j, :], RS[:, j, :], ACT.Tanh, scale=d1(NC8 + LB * n + j))
                last.then_inc(tanh_ready, 1)
                act.wait_ge(garg_ready, n + 1)
                nc.scalar.activation(SIG[:, :, :], ARG[:, :, :], ACT.Sigmoid, scale=1.5957691216057308).then_inc(gsig_ready, 1)
                if n == LH - 1:
                    split_tile("mgate", 2)
                ln_exp_tables()
                for j in range(LB):
                    last = nc.scalar.activation(AD[:, j, :], RS[:, j, :], ACT.Exp, scale=d1(C8 + LB * n + j))
                last.then_inc(decay_ready, 1)
                act.wait_ge(th_ready, n + 1)
                nc.scalar.activation(W[:, :, :], TH[:, :, :], ACT.Ln, bias=1.0)
                nc.scalar.activation(TH[:, :, :], TH[:, :, :], ACT.Ln, scale=2.0).then_inc(lns_ready, 1)
                act.wait_ge(w_ready, n + 1)
                nc.scalar.activation(W[:, :, :], W[:, :, :], ACT.Exp, scale=0.5).then_inc(mult_ready, 1)
            split_tile("mproj", 0)

            for m in range(KC):
                act.wait_ge(tile_done, TILE["mgate", m] + 1)
                if m >= 3:
                    act.wait_ge(m_ready, m - 2)
                nc.scalar.activation(msig[m % 3], PSB[2 * (m % 4)][:, :], ACT.Sigmoid).then_inc(msig_ready, 1)
                if 2 <= m < KC - 1:
                    split_tile("mgate", m + 1)
                if m >= 2:
                    split_tile("mproj", m - 1)
            split_tile("mproj", KC - 1)

            ln_exp_tables()
            for a in range(TA):
                act.wait_ge(x1_ready, 2 * a + 2)
                rstd(xn[:, a, :], 2 + a, junk).then_inc(ssq_ready, 1)
                act.wait_ge(negmax_ready, a + 1)
                nc.scalar.activation(e4[:, a, 0:TOPK], top[:, a, 0:TOPK], ACT.Exp, bias=e4[:, a, 4:5],
                                     accum_out=e4[:, a, 5:6]).then_inc(e4_ready, 1)
            act.wait_ge(gT_done, 1)
            nc.scalar.activation(gT[:, :], PSB[4][:, 0:T], ACT.Copy).then_inc(gT_ready, 1)

            def expert(it):
                act.wait_ge(glu_ready, it + 1)
                nc.scalar.activation(sg[:, :], glu[:, :], ACT.Sigmoid, scale=ALPHA).then_inc(sig_ready, 1)
                act.wait_ge(gT_done, it + 2)
                nc.scalar.activation(gT[:, :], PSB[6][:, 0:T], ACT.Copy).then_inc(gT_ready, 1)
                act.wait_ge(tile_done, it * E_TILES + (MIX_TILES + E_TILES))
                nc.scalar.activation(ysb[:, :], PSB[6][:, :], ACT.Copy).then_inc(y_ready, 1)

            with act.Fori(0, NE) as e:
                expert(e)
            act.wait_ge(route_ready, 1)
            n = act.value_load(cnt[0:1, 0:1], min_val=0, max_val=T)
            with act.If(n > SLOTS):
                with act.Fori(1, PASSES) as p:
                    with act.Fori(0, NE) as e:
                        expert(p * NE + e)

            ln_exp_tables()
            for a in range(TA):
                act.wait_ge(x2_ready, 2 * a + 2)
                rstd(x_t[:, a, :], 4 + a, xn[:, a, :]).then_inc(frs_ready, 1)

        @block.vector
        def _(dve):
            V = nc.vector
            chain = {"sem": dve_step, "n": 0}

            def link(ins):
                chain["n"] += 1
                ins.then_inc(chain["sem"], 1)
                dve.wait_ge(chain["sem"], chain["n"])

            link(V.memset(eps_t[:, :], EPS))
            link(V.memset(sc_sb[:, :, :], 0.0))
            link(V.memset(gT[:, :], 0.0))
            V.memset(xpad[:, :, 0:CONV - 1], 0.0).then_inc(vec_ready, 1)

            def normed(src, c, a):
                dve.wait_ge(ssq_ready, c + a + 1)
                V.tensor_scalar(xn[:, a, :], src[:, a, :], ss[:, c + a:c + a + 1], None, ALU.mult).then_inc(xn_ready, 1)

            for a in range(TA):
                normed(x_t, 0, a)
            dve.wait_ge(vec_in, 16)
            lam = vec[:, C_LAM:C_LAM + 8]
            c8 = lambda c: dv[:, c:c + 8]
            link(V.tensor_scalar(c8(T0), lam, -1.0, None, ALU.mult))
            link(V.tensor_tensor(c8(Y8), lam, c8(T0), ALU.max))
            V.tensor_tensor(c8(LBV), vec[:, C_LB0:C_LB0 + 8], vec[:, C_LB1:C_LB1 + 8], ALU.subtract).then_inc(vec_ready, 1)

            def fill_hT(dst, a, kb, bank, c_norm, count):
                dve.wait_ge(xT_done, count)
                w = vec[:, c_norm + 4 * kb:c_norm + 4 * kb + 4].unsqueeze(2).to_broadcast([P, 4, P])
                V.tensor_tensor(dst[:, 4 * kb:4 * kb + 4, a * P:(a + 1) * P],
                                PSB[bank][:, :].rearrange("p (k t) -> p k t", k=4), w, ALU.mult).then_inc(hT_ready, 1)

            dve.wait_ge(xn_ready, TA)
            for i in range(4):
                kb, a = i // 2, i % 2
                fill_hT(hT_f, a, kb, 4 + 2 * a + kb, C_NMIX, i + 1)
            for i in range(4):
                kb, a = i // 2, i % 2
                piece = (slice(None), slice(4 * kb, 4 * kb + 4), slice(a * P, (a + 1) * P))
                dve.wait_ge(hT_hi_ready, i + 1)
                V.tensor_tensor(hT_s[1][piece], hT_f[piece], hT_s[0][piece].bitcast(f32), ALU.subtract).then_inc(hT_lo_ready, 1)
            dve.wait_ge(lam_y, 2)
            link(V.tensor_scalar(c8(LBV), c8(LBV), 1.0, None, ALU.add))
            link(V.reciprocal(c8(LBV), c8(LBV)))
            link(V.tensor_scalar(c8(OML), c8(LBV), -1.0, 1.0, ALU.mult, ALU.add))

            link(V.tensor_scalar(c8(T1), c8(Y8), 2.0, None, ALU.add))
            link(V.reciprocal(c8(T1), c8(T1)))
            link(V.tensor_tensor(c8(T1), c8(Y8), c8(T1), ALU.mult))
            link(V.tensor_tensor(c8(T2), c8(T1), c8(T1), ALU.mult))
            link(V.memset(c8(T3), 1.0 / 17))
            for m in (15, 13, 11, 9, 7, 5, 3, 1):
                link(V.tensor_tensor(c8(T3), c8(T3), c8(T2), ALU.mult))
                link(V.tensor_scalar(c8(T3), c8(T3), 1.0 / m, None, ALU.add))
            link(V.tensor_tensor(c8(T3), c8(T3), c8(T1), ALU.mult))
            link(V.tensor_scalar(c8(T0), c8(T0), 0.0, None, ALU.max))
            link(V.scalar_tensor_tensor(c8(T3), c8(T3), 2.0, c8(T0), ALU.mult, ALU.add))
            link(V.tensor_scalar(c8(NC8), c8(T3), RG_C, None, ALU.mult))
            V.tensor_scalar(c8(C8), c8(T3), -RG_C, None, ALU.mult).then_inc(vec_ready, 1)

            def split_out(dst, ks, src):
                link(V.tensor_copy(dst[0][:, ks, :], src))
                return V.tensor_tensor(dst[1][:, ks, :], src, dst[0][:, ks, :].bitcast(f32), ALU.subtract)

            dve.wait_ge(causal_in, 16)
            dve.wait_ge(consts_in, 16)
            S = scr
            for h in range(HEADS + 2):
                p, pp = h - 1, h - 2
                if h % 2 == 0 and 2 <= h <= HEADS:
                    dve.wait_ge(sigg_ready, h // 2)
                    V.tensor_tensor(gs[:, :], PSB[3][:, :], gs[:, :], ALU.mult).then_inc(gs_ready, 1)
                if h < HEADS:
                    dve.wait_ge(sigq_ready, h + 1)
                    if h >= 1:
                        dve.wait_ge(kq_ready, h)
                    V.tensor_tensor(S["qs"][:, :], PSB[0][:, 0:T], S["sigq"][:, :], ALU.mult).then_inc(qs_ready, 1)
                if 0 <= p < HEADS:
                    dve.wait_ge(st1_done, p + 1)
                    if p >= 1:
                        dve.wait_ge(o_done, p)
                    for a in range(TA):
                        V.copy_predicated(sc_sb[:, a, :], causal_m[:, :], PSB[4][:, a * P:(a + 1) * P])
                    V.tensor_copy(kdT[:, :, :], PSB[5][:, 0:T].rearrange("p (a n) -> p a n", a=TA)).then_inc(sc_ready, 1)
                if h < HEADS:
                    dve.wait_ge(sigf_ready, h + 1)
                    if h >= 1:
                        dve.wait_ge(lnf_ready, h)
                    V.tensor_scalar(S["f"][:, :], S["sigf"][:, :], d1(OML + h), d1(LBV + h), ALU.mult, ALU.add).then_inc(f_ready, 1)
                    dve.wait_ge(f_ready, h + 1)
                    V.tensor_scalar(S["k"][:, :], S["f"][:, :], -1.0, 1.0, ALU.mult, ALU.add)
                if 0 <= p < HEADS:
                    dve.wait_ge(st2_done, p + 1)
                    link(V.tensor_copy(S_sb[:, 0, :], PSB[4][:, 0:P]))
                    link(V.scalar_tensor_tensor(S_sb[:, 1, :], S_sb[:, 0, :], decs[p % 2][:, 1:2], PSB[5][:, 0:P], ALU.mult, ALU.add))
                    V.scalar_tensor_tensor(S_sb[:, 2, :], S_sb[:, 1, :], decs[p % 2][:, 2:3], PSB[4][:, P:2 * P],
                                           ALU.mult, ALU.add).then_inc(state_ready, 1)
                if h < HEADS:
                    dve.wait_ge(lnf_ready, h + 1)
                    if h >= 1:
                        dve.wait_ge(exps_ready, h)
                    link(V.tensor_tensor_scan(S["bcum"][:, :], reset_m, S["lnf"][:, :], 0.0, ALU.mult, ALU.add))
                    b3 = S["bcum"][:, :].rearrange("p (n c) -> p n c", c=CH)
                    V.tensor_tensor(S["dlast"][:, :].rearrange("p (n c) -> p n c", c=CH),
                                    b3[:, :, CH - 1:CH].to_broadcast([P, NCH, CH]), b3, ALU.subtract).then_inc(bcum_ready, 1)
                if pp >= 0:
                    dve.wait_ge(r_ready, pp + 1)
                    dve.wait_ge(gs_ready, pp // 2 + 1)
                    link(V.tensor_tensor(o_sb[pp % 2][:, :], o_sb[pp % 2][:, :], S["rinv"][:, :], ALU.mult))
                    link(V.scalar_tensor_tensor(o_sb[pp % 2][:, :], o_sb[pp % 2][:, :], v1(C_GN + pp),
                                                gs[:, (pp % 2) * T:(pp % 2 + 1) * T],
                                                ALU.mult, ALU.mult))
                    split_out(oA_s, slice(pp, pp + 1), o_sb[pp % 2][:, :].unsqueeze(1)).then_inc(oA_ready, 1)
                if h < HEADS:
                    dve.wait_ge(exps_ready, h + 1)
                if 0 <= p < HEADS:
                    dve.wait_ge(o_done, p + 1)
                    if p >= 2:
                        dve.wait_ge(oA_ready, p - 1)
                    V.tensor_copy(o_sb[p % 2][:, :], PSB[7][:, 0:T]).then_inc(o_copied, 1)
                if h < HEADS:
                    V.tensor_copy(decs[h % 2][:, :], S["eb"][:, CH - 1::CH])
                    V.tensor_tensor(q_in[:, :], S["qs"][:, :], S["eb"][:, :], ALU.mult)
                    V.tensor_tensor(k_in[:, :], S["k"][:, :], S["enb"][:, :], ALU.mult)
                    V.tensor_tensor(k_dec[:, :], S["k"][:, :], S["edec"][:, :], ALU.mult).then_inc(kq_ready, 1)

            XSQ, ARG, SIG, RS, IG, AD, TH, W = LR

            def convolve(n):
                x_c = xc[n % 2]
                dve.wait_ge(xb_copied, n + 1)
                if n >= 2:
                    dve.wait_ge(tile_done, TILE["rg", n - 2] + 1)
                for k in range(CONV):
                    for b in range(LB):
                        c = LB * n + b
                        if k == 0:
                            last = V.tensor_scalar(x_c[:, b, :], xpad[:, b, 0:T], v1(C_CW + c), v1(C_CB + c), ALU.mult, ALU.add)
                        else:
                            last = V.scalar_tensor_tensor(x_c[:, b, :], xpad[:, b, k:k + T], v1(C_CW + 8 * k + c),
                                                          x_c[:, b, :], ALU.mult, ALU.add)
                    if k < CONV - 1:
                        link(last)
                    else:
                        last.then_inc(xc_ready, 1)

            convolve(0)
            for n in range(LH):
                bk = 4 * (n % 2)
                gate_ps = PSB[bk + 1][:, :].rearrange("p (b n) -> p b n", b=LB)
                dve.wait_ge(gsq_ready, n + 1)
                link(V.tensor_scalar(XSQ[:, :, :], XSQ[:, :, :], 0.044715, 1.0, ALU.mult, ALU.add))
                V.tensor_tensor(ARG[:, :, :], gate_ps, XSQ[:, :, :], ALU.mult).then_inc(garg_ready, 1)
                if n + 1 < LH:
                    convolve(n + 1)
                dve.wait_ge(tanh_ready, n + 1)
                V.tensor_scalar(TH[:, :, :], TH[:, :, :], 2.0 ** -64, None, ALU.max).then_inc(th_ready, 1)
                dve.wait_ge(gsig_ready, n + 1)
                link(V.tensor_tensor(SIG[:, :, :], gate_ps, SIG[:, :, :], ALU.mult))
                dve.wait_ge(rsig_ready, n + 1)
                link(V.tensor_tensor(IG[:, :, :], xc[n % 2][:, :, :], IG[:, :, :], ALU.mult))
                dve.wait_ge(lns_ready, n + 1)
                V.tensor_tensor(W[:, :, :], TH[:, :, :], W[:, :, :], ALU.subtract).then_inc(w_ready, 1)
                dve.wait_ge(mult_ready, n + 1)
                link(V.memset(W[:, :, 0:1], 1.0))
                link(V.tensor_tensor(IG[:, :, :], IG[:, :, :], W[:, :, :], ALU.mult))
                dve.wait_ge(decay_ready, n + 1)
                for j in range(LB):
                    last = V.tensor_tensor_scan(ARG[:, j, :], AD[:, j, :], IG[:, j, :], 0.0, ALU.mult, ALU.add)
                link(last)
                link(V.tensor_tensor(ARG[:, :, :], ARG[:, :, :], SIG[:, :, :], ALU.mult))
                split_out(oB_s, slice(LB * n, LB * (n + 1)), ARG[:, :, :]).then_inc(oB_ready, 1)

            for m in range(KC):
                dve.wait_ge(msig_ready, m + 1)
                dve.wait_ge(tile_done, TILE["mproj", m] + 1)
                s2 = msig[m % 3]
                link(V.tensor_tensor(s2, PSB[1 + 2 * (m % 4)][:, :], s2, ALU.mult))
                V.tensor_tensor(merged[:, m, :], s2[:, 0:T], s2[:, T:2 * T], ALU.add).then_inc(m_ready, 1)

            V.memset(gsel[:, :, :], 0.0)

            def residual(a):
                dve.wait_ge(*((yo_done, 1) if a == 0 else (tile_done, MIX_TILES)))
                dve.wait_ge(x_again, 32)
                for n2 in range(2):
                    c = slice(n2 * 512, (n2 + 1) * 512)
                    V.tensor_tensor(xn[:, a, c], PSB[2 * a + n2][:, :], x_t[:, a, c], ALU.add).then_inc(x1_ready, 1)
                dve.wait_ge(x1_ready, 2 * a + 2)

            dve.wait_ge(router_in, 32)
            iota_k = iota_m[:, 0:NE].unsqueeze(1).to_broadcast([P, TOPK, NE])

            def choose(a):
                dve.wait_ge(lg_done, a + 1)
                dve.wait_ge(ssq_ready, TA + a + 1)
                link(V.scalar_tensor_tensor(lg[:, a, :], PSB[7 - a][:, 0:NE], ss[:, 2 + a:3 + a], br[:, :], ALU.mult, ALU.add))
                link(V.max(top[:, a, :], lg[:, a, :]))
                V.tensor_scalar(e4[:, a, 4:5], top[:, a, 0:1], -1.0, None, ALU.mult).then_inc(negmax_ready, 1)
                link(V.max_index(topi[:, a, :], top[:, a, :], lg[:, a, :]))
                link(V.tensor_copy(topf[:, a, :], topi[:, a, :]))
                link(V.tensor_tensor(oneh[:, :, :], iota_k, topf[:, a, 0:TOPK].unsqueeze(2).to_broadcast([P, TOPK, NE]),
                                     ALU.is_equal))
                V.tensor_reduce(mask[:, a, :], oneh[:, :, :].rearrange("p k e -> p e k"), AX.X, ALU.add).then_inc(mask_ready, 1)

            def weigh(a):
                dve.wait_ge(e4_ready, a + 1)
                dve.wait_ge(mask_ready, a + 1)
                link(V.reciprocal(e4[:, a, 5:6], e4[:, a, 5:6]))
                link(V.tensor_tensor(oneh[:, :, :], oneh[:, :, :], e4[:, a, 0:TOPK].unsqueeze(2).to_broadcast([P, TOPK, NE]),
                                     ALU.mult))
                link(V.tensor_reduce(gate[:, a, :], oneh[:, :, :].rearrange("p k e -> p e k"), AX.X, ALU.add))
                link(V.tensor_scalar(gates[:, a, 0:NE], gate[:, a, :], e4[:, a, 5:6], None, ALU.mult))
                V.tensor_copy(gsel[:, a, :].rearrange("p (h e) -> p h e", h=2)[:, :, 0:NE],
                              gates[:, a, 0:NE].unsqueeze(1).to_broadcast([P, 2, NE])).then_inc(gated, 1)

            for a in range(TA):
                residual(a)
                for kb in range(2):
                    fill_hT(hT, a, kb, 4 + 2 * a + kb, C_NFFN, 2 * (TA + a) + kb + 1)
                choose(a)
                weigh(a)
                normed(xn, 2, a)
            dve.wait_ge(rank_done, 1)
            rank2 = ranks[:, :, 0:NE]
            link(V.scalar_tensor_tensor(rank2, PSB[7][:, 0:TA * NE].rearrange("p (a e) -> p a e", a=TA), 1.0, mask[:, :, :],
                                        ALU.add, ALU.mult))
            link(V.tensor_scalar(rank2, rank2, -1.0, None, ALU.add))

            STEPS = 2
            nffn_b = vec[:, C_NFFN:C_NFFN + KC].unsqueeze(2).to_broadcast([P, KC, SLOTS])

            def expert(it, e):
                chain = [it * STEPS]

                def link(ins):
                    chain[0] = chain[0] + 1
                    ins.then_inc(moe_step, 1)
                    dve.wait_ge(moe_step, chain[0])

                for a in range(TA):
                    last = V.tensor_scalar(sel[:, a, :], iota_m[:, 0:SLOTS], ranks[:, a, bass.ds(it, 1)], None, ALU.is_equal)
                last.then_inc(sel_ready, 1)
                V.tensor_scalar(oh[:, :], ident[0:NE, bass.ds(e, 1)].to_broadcast([NE, SLOTS]), 1.0, None,
                                ALU.mult).then_inc(oh_ready, 1)
                dve.wait_ge(gT_ready, it + 1)
                for a in range(TA):
                    last = V.tensor_scalar(gsel[:, a, :], iota_m, ranks[:, a, bass.ds(it, 1)],
                                           gates[:, a, bass.ds(it, 1)], ALU.is_equal, ALU.mult)
                last.then_inc(gsel_ready, 1)
                for half in range(2):
                    ks = slice(half * KC // 2, (half + 1) * KC // 2)
                    dve.wait_ge(gath_done, 2 * it + half + 1)
                    V.tensor_tensor(xs[:, ks, :], PSB[7][:, :].rearrange("p (k s) -> p k s", k=KC)[:, ks, :], nffn_b[:, ks, :],
                                    ALU.mult).then_inc(xs_ready, 1)
                dve.wait_ge(tile_done, it * E_TILES + (MIX_TILES + KC))
                V.tensor_scalar(glu, PSB[4][:, :], LIMIT, None, ALU.min).then_inc(glu_ready, 1)
                link(V.tensor_scalar(lin, PSB[5][:, :], LIMIT, -LIMIT, ALU.min, ALU.max))
                dve.wait_ge(glu_ready, it + 1)
                link(V.scalar_tensor_tensor(lin, lin, 1.0, glu, ALU.add, ALU.mult))
                dve.wait_ge(sig_ready, it + 1)
                V.tensor_tensor(ac, lin, sg, ALU.mult).then_inc(act_ready, 1)
                dve.wait_ge(actT_done, it + 1)
                V.tensor_copy(acT[:, :, :, :].rearrange("p c h s -> p (c h s)"), PSB[4][:, :]).then_inc(actT_ready, 1)

            dve.wait_ge(count_done, 1)
            V.reduce_max(cmax[:, :], PSB[6][:, 0:NE], AX.X).then_inc(count_read, 1)
            dve.wait_ge(count_read, 1)
            V.tensor_copy(cnt[:, :], cmax[:, :]).then_inc(route_ready, 1)
            with dve.Fori(0, NE) as e:
                expert(e, e)
            dve.wait_ge(route_ready, 1)
            n = dve.value_load(cnt[0:1, 0:1], min_val=0, max_val=T)
            with dve.If(n > SLOTS):
                for q in range(1, PASSES):
                    V.tensor_scalar(ranks[:, :, q * NE:(q + 1) * NE], rank2, float(-SLOTS * q), None, ALU.add)
                    last = V.tensor_copy(gates[:, :, q * NE:(q + 1) * NE], gates[:, :, 0:NE])
                last.then_inc(route_ready, 1)
                dve.wait_ge(route_ready, 2)
                with dve.Fori(1, PASSES) as p:
                    with dve.Fori(0, NE) as e:
                        expert(p * NE + e, e)

            dve.wait_ge(moe_in, 32)
            for a in range(TA):
                dve.wait_ge(moe_done, a + 1)
                for n2 in range(2):
                    c = slice(n2 * 512, (n2 + 1) * 512)
                    V.tensor_tensor(x_t[:, a, c], PSB[2 * a + n2][:, :], x_t[:, a, c], ALU.add).then_inc(x2_ready, 1)
            for a in range(TA):
                dve.wait_ge(frs_ready, a + 1)
                V.scalar_tensor_tensor(xn[:, a, :], x_t[:, a, :], ss[:, 4 + a:5 + a], nfin, ALU.mult,
                                       ALU.mult).then_inc(fin_ready, 1)


def constants():
    c = np.zeros((P, K_END), np.float32)
    c[:, K_ID:K_ID + P] = np.eye(P)
    c[:, K_MEAN:K_MEAN + P] = 1.0 / P
    c[:, K_RESET:K_RESET + T] = np.arange(T) % CH != 0
    c[:, K_IOTA:K_IOTA + P] = np.arange(P) % SLOTS
    c[:, K_TRI:K_TRI + P] = np.triu(np.ones((P, P)), 1)
    c[:, K_ONE:K_ONE + P] = 1.0
    j, i = np.arange(P)[:, None], np.arange(P)[None, :]
    causal = ((i >= j) & (i // CH == j // CH)).astype(np.int32)
    return c, causal


def kernel(**inputs):
    import concourse.bacc as bacc
    from concourse.bass_utils import run_bass_kernel_spmd

    i = {k: np.asarray(v) for k, v in inputs.items()}

    def cols(v):
        return v.reshape(-1, P).T

    vecs = np.concatenate([cols(i[n]) for n in ("norm_mix", "norm_ffn", "gn_w", "conv_w", "conv_b", "b_rg_a", "b_rg_x",
                                                 "lru_lambda", "lb_raw")], axis=1)

    def block(w, c):
        return w[:, c * P:(c + 1) * P].reshape(KC, P, P).transpose(1, 0, 2).reshape(P, D)

    w_in = i["w_in"][0]
    q, f, v, g, xb, gb, ga, gbb = (8 * n for n in range(8))

    def tile(kind, n):
        if kind == "qf":
            return block(w_in, q + n), block(w_in, f + n)
        if kind == "vv":
            return (w_in[:, (v + 2 * n) * P:(v + 2 * n + 2) * P].reshape(KC, P, 2 * P).transpose(1, 0, 2).reshape(P, 2 * D),)
        if kind == "gg":
            return block(w_in, g + 2 * n), block(w_in, g + 2 * n + 1)
        if kind in ("xb", "gate"):
            c = (xb if kind == "xb" else gb) + LB * n
            return block(w_in, c), block(w_in, c + 1)
        if kind == "rg":
            rg = [i[w][0, n].reshape(LB, P, LB * P).transpose(1, 0, 2).reshape(P, 512) for w in ("w_rg_a", "w_rg_x")]
            return (*rg, np.zeros((P, D), np.float32))
        if kind == "mgate":
            return block(w_in, ga + n), block(w_in, gbb + n)
        if kind == "mproj":
            return block(i["w_proj_a"][0], n), block(i["w_proj_b"][0], n)
        w = i["w_out"][0]
        return w[2 * n * P:(2 * n + 1) * P], w[(2 * n + 1) * P:(2 * n + 2) * P]

    tiles = [tile(*name) for name in ORDER]
    mixw = np.stack([np.concatenate(t, axis=1) for t in tiles])

    w_gu = i["w_gu"][0].reshape(NE, KC, P, D, 2).transpose(0, 1, 2, 4, 3).reshape(NE, KC, P, 2 * D)
    b_gu = i["b_gu"][0].reshape(NE, D, 2).transpose(0, 2, 1).reshape(NE, 2 * D)
    b_down = np.zeros((2, SLOTS, 512), np.float32)
    b_down[:, :NE] = i["b_down"][0].reshape(NE, 2, 512).transpose(1, 0, 2)
    b_down = b_down.reshape(P, 512)
    consts, causal = constants()
    arrays = {
        "x": i["x"][0].reshape(TA, P, D).transpose(1, 0, 2),
        "vecs": vecs, "consts": consts, "causal": causal, "mixw": mixw,
        "w_router": i["w_router"][0].reshape(KC, P, NE).transpose(1, 0, 2),
        "b_router": np.tile(i["b_router"], (P, 1)),
        "w_gu": w_gu, "b_gu": b_gu, "w_down": i["w_down"][0], "b_down": b_down,
        "norm_final": np.tile(i["norm_final"][None], (P, 1)),
    }
    arrays = {f"in_{k}": np.ascontiguousarray(a) for k, a in arrays.items()}
    nc = bacc.Bacc("TRN2", target_bir_lowering=False, num_devices=1)
    args = [nc.dram_tensor(k, a.shape, mybir.dt.from_np(a.dtype), kind="ExternalInput").ap() for k, a in arrays.items()]
    args.append(nc.dram_tensor("out_y", (T, D), mybir.dt.float32, kind="ExternalOutput").ap())
    build(nc, *args)
    r = run_bass_kernel_spmd(nc, [arrays], core_ids=[0])
    return r.results[0]["out_y"].reshape(1, T, D)
```
